# Optimizing a Trainium2 kernel written in Bass

```python
import jax, jax.numpy as jnp
from jax import lax
import numpy as np

D_MODEL = 1024
BATCH = 1
SEQ = 512
DEPTH = 1
DEC_BATCH = 8
DEC_SEQ = 1
PAST_LEN = 4096
PAGE_SIZE = 128

MIX_WIDTH = D_MODEL
POOL_WIDTH = MIX_WIDTH // 2
POOL_GROUPS = 4
POOL_GROUP_DIM = POOL_WIDTH // POOL_GROUPS
POOL_WINDOWS = (2, 4, 8, 16)
POOL_BUF = max(POOL_WINDOWS) - 1
MLSTM_WIDTH = MIX_WIDTH - POOL_WIDTH
MLSTM_HEADS = 4
MLSTM_HEAD_DIM = MLSTM_WIDTH // MLSTM_HEADS
MLSTM_CHUNK = 64
N_MEM = 256
CA_HEADS = 4
CA_HEAD_DIM = D_MODEL // CA_HEADS
N_GROUPS = 4
EXPERTS_PER_GROUP = 4
N_EXPERTS = N_GROUPS * EXPERTS_PER_GROUP
TOP_K = 2
D_EXPERT = D_MODEL // 4
ALPHA = (2 * DEPTH) ** 0.25
BETA = (8 * DEPTH) ** -0.25
LN_EPS = 1e-5
GATE_OFF = POOL_WIDTH + 4 * MLSTM_WIDTH
IN_COLS = GATE_OFF + 2 * MLSTM_HEADS

kernel_name = "hymba_pool_mlstm_memxattn_hmoe_step"

F32 = jnp.float32

def layer_norm(x, g, b):
    xf = x.astype(F32)
    mu = xf.mean(-1, keepdims=True)
    var = jnp.mean(jnp.square(xf - mu), -1, keepdims=True)
    y = (xf - mu) * lax.rsqrt(var + LN_EPS)
    return (y * g.astype(F32) + b.astype(F32)).astype(x.dtype)

def pool_mix(u, prev, pool_w, pool_scale):
    B, T, C = u.shape
    P = prev.shape[1]
    ext = jnp.concatenate([prev.astype(F32), u.astype(F32)], axis=1)
    cs = jnp.concatenate([jnp.zeros((B, 1, C), F32), jnp.cumsum(ext, axis=1)], axis=1)
    hi = P + 1 + jnp.arange(T)
    outs = []
    for g, w in enumerate(POOL_WINDOWS):
        lo = jnp.maximum(hi - w, 0)
        sl = slice(g * POOL_GROUP_DIM, (g + 1) * POOL_GROUP_DIM)
        csg = cs[..., sl]
        cnt = (hi - lo).astype(F32)[None, :, None]
        diff = (csg[:, hi] - csg[:, lo]) / cnt - ext[:, P:, sl]
        outs.append(jnp.einsum('btc,ce->bte', diff, pool_w[g].astype(F32)))
    y = jnp.concatenate(outs, -1) * pool_scale.astype(F32)
    return y.astype(u.dtype), ext[:, -POOL_BUF:].astype(u.dtype)

def mlstm_chunk(state, inp):
    C, n, m = state
    q, k, v, ig, lf = inp
    L = q.shape[2]
    b = jnp.cumsum(lf, axis=-1)
    inter = b + m[..., None]
    causal = jnp.tril(jnp.ones((L, L), dtype=bool))
    dmat = jnp.where(causal, b[..., :, None] - b[..., None, :] + ig[..., None, :], -jnp.inf)
    m_t = jnp.maximum(inter, dmat.max(-1))
    w_intra = jnp.exp(dmat - m_t[..., None])
    w_inter = jnp.exp(inter - m_t)
    s = jnp.einsum('bhjd,bhsd->bhjs', q, k) * w_intra
    num = jnp.einsum('bhjs,bhsv->bhjv', s, v) + w_inter[..., None] * jnp.einsum('bhvd,bhjd->bhjv', C, q)
    qn = s.sum(-1) + w_inter * jnp.einsum('bhd,bhjd->bhj', n, q)
    h = num / jnp.maximum(jnp.abs(qn), jnp.exp(-m_t))[..., None]
    m_new = m_t[..., -1]
    w_state = jnp.exp(b[..., -1:] - b + ig - m_new[..., None])
    decay = jnp.exp(b[..., -1] + m - m_new)
    C_new = decay[..., None, None] * C + jnp.einsum('bhs,bhsv,bhsd->bhvd', w_state, v, k)
    n_new = decay[..., None] * n + jnp.einsum('bhs,bhsd->bhd', w_state, k)
    return (C_new, n_new, m_new), h

def mlstm_seq(q, k, v, ig, lf, C0, n0, m0):
    B, H, T, _ = q.shape
    L = MLSTM_CHUNK if T % MLSTM_CHUNK == 0 else T
    nc = T // L

    def to_chunks(a):
        a = a.reshape(a.shape[:2] + (nc, L) + a.shape[3:])
        return jnp.moveaxis(a, 2, 0)

    state, h = lax.scan(mlstm_chunk, (C0, n0, m0), tuple(to_chunks(a) for a in (q, k, v, ig, lf)))
    h = jnp.moveaxis(h, 0, 2).reshape(B, H, T, -1)
    return h, state

def hier_moe(x, p):
    B, T, D = x.shape
    xf = x.reshape(B * T, D)
    g_logits = (xf @ p['w_gr']).astype(F32) + p['b_gr'].astype(F32)
    pg = jax.nn.softmax(g_logits, -1)
    g_sel = jnp.argmax(g_logits, -1)
    e_logits = ((xf @ p['w_er']).astype(F32) + p['b_er'].astype(F32)).reshape(-1, N_GROUPS, EXPERTS_PER_GROUP)
    e_in = jnp.take_along_axis(e_logits, g_sel[:, None, None], axis=1)[:, 0]
    top_p, top_i = lax.top_k(jax.nn.softmax(e_in, -1), TOP_K)
    gate = jnp.take_along_axis(pg, g_sel[:, None], 1) * top_p / top_p.sum(-1, keepdims=True)
    e_idx = g_sel[:, None] * EXPERTS_PER_GROUP + top_i
    combine = jnp.einsum('nk,nke->ne', gate, jax.nn.one_hot(e_idx, N_EXPERTS, dtype=F32)).astype(x.dtype)
    hg = jnp.einsum('nd,edf->nef', xf, p['w_gate'])
    hu = jnp.einsum('nd,edf->nef', xf, p['w_up'])
    hh = jax.nn.silu(hg) * hu * combine[..., None]
    y = jnp.einsum('nef,efd->nd', hh, p['w_down'])
    return y.reshape(B, T, D)

def trunk_layer(x, mem_k, mem_v, pool_prev, C0, n0, m0, p):
    B, T, _ = x.shape
    h = jnp.einsum('btd,de->bte', x, p['w_in'])
    u = h[..., :POOL_WIDTH]
    q, k, v, og = [h[..., POOL_WIDTH + i * MLSTM_WIDTH: POOL_WIDTH + (i + 1) * MLSTM_WIDTH] for i in range(4)]
    ig = h[..., GATE_OFF:GATE_OFF + MLSTM_HEADS].astype(F32) + p['b_i'].astype(F32)
    fg = h[..., GATE_OFF + MLSTM_HEADS:].astype(F32) + p['b_f'].astype(F32)
    pool_out, pool_buf = pool_mix(u, pool_prev, p['pool_w'], p['pool_scale'])

    def heads(a):
        return a.reshape(B, T, MLSTM_HEADS, MLSTM_HEAD_DIM).transpose(0, 2, 1, 3).astype(F32)

    hm, (C1, n1, m1) = mlstm_seq(heads(q) * MLSTM_HEAD_DIM ** -0.5, heads(k), heads(v),
                                 ig.transpose(0, 2, 1), jax.nn.log_sigmoid(fg).transpose(0, 2, 1),
                                 C0.astype(F32), n0.astype(F32), m0.astype(F32))
    mu = hm.mean(-1, keepdims=True)
    var = jnp.mean(jnp.square(hm - mu), -1, keepdims=True)
    hn = ((hm - mu) * lax.rsqrt(var + LN_EPS)).transpose(0, 2, 1, 3).reshape(B, T, MLSTM_WIDTH)
    mlstm_out = (jax.nn.sigmoid(og.astype(F32)) * hn * p['mlstm_norm_g'].astype(F32)).astype(x.dtype)
    mix = jnp.einsum('bte,ed->btd', jnp.concatenate([pool_out, mlstm_out], -1), p['w_out'])
    x = layer_norm(ALPHA * x + mix, p['ln1_g'], p['ln1_b'])

    qc = (x @ p['ca_wq']).reshape(B, T, CA_HEADS, CA_HEAD_DIM)
    sc = jnp.einsum('bthe,bmhe->bhtm', qc.astype(F32), mem_k.astype(F32)) * CA_HEAD_DIM ** -0.5
    pa = jax.nn.softmax(sc, -1)
    ctx = jnp.einsum('bhtm,bmhe->bthe', pa, mem_v.astype(F32)).reshape(B, T, D_MODEL).astype(x.dtype)
    x = layer_norm(ALPHA * x + ctx @ p['ca_wo'], p['ln2_g'], p['ln2_b'])

    x = layer_norm(ALPHA * x + hier_moe(x, p), p['ln3_g'], p['ln3_b'])
    return x, pool_buf, C1, n1, m1

def setup_inputs(seed: int = 0) -> dict:
    key = jax.random.key(seed)
    ks = iter(jax.random.split(key, 48))

    def nrm(shape, scale):
        return jax.random.normal(next(ks), shape, F32) * scale

    def gain(shape):
        return 1.0 + nrm(shape, 0.1)

    pool_buf_len = min(POOL_BUF, PAST_LEN)
    L, D = DEPTH, D_MODEL
    return {
        'x_prompt': nrm((BATCH, SEQ, D), 1.0),
        'x_sample': nrm((DEC_BATCH, DEC_SEQ, D), 1.0),
        'mem_prompt': nrm((BATCH, N_MEM, D), 1.0),
        'cache_pool': nrm((L, DEC_BATCH, pool_buf_len, POOL_WIDTH), 1.0),
        'state_mlstm_C': nrm((L, DEC_BATCH, MLSTM_HEADS, MLSTM_HEAD_DIM, MLSTM_HEAD_DIM), 0.1),
        'state_mlstm_n': nrm((L, DEC_BATCH, MLSTM_HEADS, MLSTM_HEAD_DIM), 0.1),
        'state_mlstm_m': nrm((L, DEC_BATCH, MLSTM_HEADS), 1.0),
        'cache_mem_k': nrm((L, DEC_BATCH, N_MEM, CA_HEADS, CA_HEAD_DIM), 1.0),
        'cache_mem_v': nrm((L, DEC_BATCH, N_MEM, CA_HEADS, CA_HEAD_DIM), BETA),
        'emb_ln_g': gain((D,)),
        'emb_ln_b': nrm((D,), 0.02),
        'w_in': nrm((L, D, IN_COLS), D ** -0.5),
        'b_i': nrm((L, MLSTM_HEADS), 0.1),
        'b_f': jnp.linspace(3.0, 6.0, MLSTM_HEADS, dtype=F32)[None] + nrm((L, MLSTM_HEADS), 0.1),
        'pool_w': nrm((L, POOL_GROUPS, POOL_GROUP_DIM, POOL_GROUP_DIM), POOL_GROUP_DIM ** -0.5),
        'pool_scale': gain((L, POOL_WIDTH)),
        'mlstm_norm_g': gain((L, MLSTM_WIDTH)),
        'w_out': nrm((L, MIX_WIDTH, D), MIX_WIDTH ** -0.5 * BETA),
        'ln1_g': gain((L, D)),
        'ln1_b': nrm((L, D), 0.02),
        'ca_wq': nrm((L, D, D), D ** -0.5),
        'ca_wk': nrm((L, D, D), D ** -0.5),
        'ca_wv': nrm((L, D, D), D ** -0.5 * BETA),
        'ca_wo': nrm((L, D, D), D ** -0.5 * BETA),
        'ln2_g': gain((L, D)),
        'ln2_b': nrm((L, D), 0.02),
        'w_gr': nrm((L, D, N_GROUPS), D ** -0.5),
        'b_gr': nrm((L, N_GROUPS), 0.01),
        'w_er': nrm((L, D, N_EXPERTS), D ** -0.5),
        'b_er': nrm((L, N_EXPERTS), 0.01),
        'w_gate': nrm((L, N_EXPERTS, D, D_EXPERT), D ** -0.5),
        'w_up': nrm((L, N_EXPERTS, D, D_EXPERT), D ** -0.5),
        'w_down': nrm((L, N_EXPERTS, D_EXPERT, D), D_EXPERT ** -0.5 * BETA),
        'ln3_g': gain((L, D)),
        'ln3_b': nrm((L, D), 0.02),
    }

def reference(x_prompt, x_sample, mem_prompt, cache_pool, state_mlstm_C, state_mlstm_n, state_mlstm_m,
              cache_mem_k, cache_mem_v, emb_ln_g, emb_ln_b, w_in, b_i, b_f, pool_w, pool_scale,
              mlstm_norm_g, w_out, ln1_g, ln1_b, ca_wq, ca_wk, ca_wv, ca_wo, ln2_g, ln2_b,
              w_gr, b_gr, w_er, b_er, w_gate, w_up, w_down, ln3_g, ln3_b):
    xp = layer_norm(x_prompt, emb_ln_g, emb_ln_b)
    xs = layer_norm(x_sample, emb_ln_g, emb_ln_b)
    B = xp.shape[0]
    p_pool, p_C, p_n, p_m, p_mk, p_mv = [], [], [], [], [], []
    s_pool, s_C, s_n, s_m = [], [], [], []
    for l in range(DEPTH):
        p = dict(w_in=w_in[l], b_i=b_i[l], b_f=b_f[l], pool_w=pool_w[l], pool_scale=pool_scale[l],
                 mlstm_norm_g=mlstm_norm_g[l], w_out=w_out[l], ln1_g=ln1_g[l], ln1_b=ln1_b[l],
                 ca_wq=ca_wq[l], ca_wo=ca_wo[l], ln2_g=ln2_g[l], ln2_b=ln2_b[l],
                 w_gr=w_gr[l], b_gr=b_gr[l], w_er=w_er[l], b_er=b_er[l],
                 w_gate=w_gate[l], w_up=w_up[l], w_down=w_down[l], ln3_g=ln3_g[l], ln3_b=ln3_b[l])
        mk = (mem_prompt @ ca_wk[l]).reshape(B, N_MEM, CA_HEADS, CA_HEAD_DIM)
        mv = (mem_prompt @ ca_wv[l]).reshape(B, N_MEM, CA_HEADS, CA_HEAD_DIM)
        pool_prev = jnp.zeros((B, 0, POOL_WIDTH), xp.dtype)
        C0 = jnp.zeros((B, MLSTM_HEADS, MLSTM_HEAD_DIM, MLSTM_HEAD_DIM), F32)
        n0 = jnp.zeros((B, MLSTM_HEADS, MLSTM_HEAD_DIM), F32)
        m0 = jnp.zeros((B, MLSTM_HEADS), F32)
        xp, pb, C1, n1, m1 = trunk_layer(xp, mk, mv, pool_prev, C0, n0, m0, p)
        p_pool.append(pb)
        p_C.append(C1.astype(state_mlstm_C.dtype))
        p_n.append(n1.astype(state_mlstm_n.dtype))
        p_m.append(m1.astype(state_mlstm_m.dtype))
        p_mk.append(mk)
        p_mv.append(mv)
        xs, sb, Cs, ns, ms = trunk_layer(xs, cache_mem_k[l], cache_mem_v[l], cache_pool[l],
                                         state_mlstm_C[l], state_mlstm_n[l], state_mlstm_m[l], p)
        s_pool.append(sb.astype(cache_pool.dtype))
        s_C.append(Cs.astype(state_mlstm_C.dtype))
        s_n.append(ns.astype(state_mlstm_n.dtype))
        s_m.append(ms.astype(state_mlstm_m.dtype))
    return (xp, xs, jnp.stack(p_pool), jnp.stack(p_C), jnp.stack(p_n), jnp.stack(p_m),
            jnp.stack(p_mk), jnp.stack(p_mv), jnp.stack(s_pool), jnp.stack(s_C), jnp.stack(s_n), jnp.stack(s_m))


_drawn_inputs = setup_inputs


def setup_inputs(seed=0):
    import zlib

    import numpy as np

    out = dict(_drawn_inputs(seed))
    spreads = {}
    factors = {'mlstm_norm_g': 2.728, 'ln1_b': 2.685, 'b_gr': 22.55, 'b_er': 25.991, 'ln3_b': 2.858}
    for name, (base, spread) in spreads.items():
        noise = np.random.default_rng([zlib.crc32(name.encode()), seed]).standard_normal(out[name].shape)
        drawn = base * np.exp(spread * noise) if base else spread * noise
        out[name] = __import__('jax').numpy.asarray(drawn.astype(out[name].dtype))
    for name, factor in factors.items():
        out[name] = (out[name] * factor).astype(out[name].dtype)
    return out
```

```python
import numpy as np
import concourse.bass as bass
from concourse import mybir
from contextlib import ExitStack

F32 = mybir.dt.float32
BF16 = mybir.dt.bfloat16
U32 = mybir.dt.uint32
I32 = mybir.dt.int32
ALU = mybir.AluOpType
ACT = mybir.ActivationFunctionType
AX = mybir.AxisListType.X

D = 1024
NP_, NS = 512, 8
NTOK = NP_ + NS
NT = 5
TR = NTOK // NT
LAST = NP_ - (NT - 1) * TR
KC = D // 128
H, HD = 4, 128
PW = 512
NPOOL = 15
NM = 256
CE = 256
NE, NG, EG = 16, 4, 4
DE = 256
C = 128
NCH = -(-NTOK // C)
R = NCH * C
WR = 3
ALPHA = 2.0 ** 0.25
LN_EPS = 1e-5
GRP = [(0, 3 * TR), (3 * TR, 2 * TR)]
COLS = 312
PADC = 16
BIG = -3.0e38


def rows_of(t):
    return LAST if t == NT - 1 else TR


def constants():
    c = np.zeros((128, COLS), np.float32)
    c[:, 0:128] = np.eye(128, dtype=np.float32)
    c[0:TR, 128:128 + TR] = np.triu(np.ones((TR, TR), np.float32), 1)
    for g in range(4):
        w = 2 << g
        c[:, 232 + 16 * g:248 + 16 * g] = 1.0 / np.minimum(np.arange(16) + 1, w)
    c[:, 296:312] = np.arange(16)
    return c


def layer_kernel(nc, a, o):
    (o_xp, o_xs, o_ppool, o_pC, o_pn, o_pm, o_pmk, o_pmv, o_spool, o_sC, o_sn, o_sm) = o
    ctx = ExitStack()
    with ctx:
        def sb(name, shape, dt=F32):
            return ctx.enter_context(nc.sbuf_tensor(name, shape, dt))

        def sem(name):
            return ctx.enter_context(nc.semaphore(name))

        def dram(name, shape, dt=F32):
            return nc.dram_tensor(name, shape, dt, kind="Internal").ap()

        qk_d = dram("qk_d", [NS, 1024])
        swc_d = dram("swc_d", [NS, H])
        sq2_d = dram("sq2_d", [NS, D])
        x2_d = dram("x2_d", [NTOK, D])
        lst_d = dram("lst_d", [NE * R, 1], U32)
        y_d = dram("y_d", [NE * R, D])
        lst_e = lst_d.rearrange("(r e) one -> r (e one)", e=NE)
        y_e = y_d.rearrange("(r e) d -> r e d", e=NE)

        xn = sb("xn", [128, NT, D])
        xT = sb("xT", [128, KC, NTOK])
        wring = sb("wring", [128, WR, KC, 512])
        con = sb("con", [128, COLS])
        gb = sb("gb", [128, 2, D])
        mkT = sb("mkT", [128, KC, NM])
        mv = sb("mv", [128, 2, D])
        poolw = sb("poolw", [128, 4, 128])
        wg = sb("wg", [128, KC, 36])
        wr = sb("wr", [128, KC, 20])
        smp = sb("smp", [128, 2560])
        colv = sb("colv", [128, 16])
        gcol = sb("gcol", [128, 48])
        wcol = sb("wcol", [128, NT, H])
        st = sb("st", [128, 12])
        agg = sb("agg", [128, 2])
        rstd = sb("rstd", [128, NT])
        half = sb("half", [128, NT])
        hst = sb("hst", [128, NT, 6])
        hagg = sb("hagg", [128, NT, 2])
        den = sb("den", [128, 2, NT])
        P = sb("P", [128, 21038])
        sg8 = sb("sg8", [NS, 64])
        onesb = sb("onesb", [TR, TR], BF16)
        trib = sb("trib", [TR, TR], BF16)
        ps = [ctx.enter_context(nc.psum_tensor(f"ps{i}", [128, 512], F32)) for i in range(8)]
        RING_A, RING_D, MBANK = ps[0:3], ps[3:6], ps[6:8]

        ident = con[:, 0:128]
        invc = con[:, 232:296].rearrange("p (g c) -> p g c", g=4)

        def view(lo, n, pat=None, **kw):
            v = P[:, lo:lo + n]
            return v.rearrange(pat, **kw) if pat else v

        uw = PADC + NTOK
        uT = view(0, 4 * uw, "p (g c) -> p g c", g=4)
        qT = view(2144, 2080, "p (h c) -> p h c", h=4)
        kT = view(4224, 2080, "p (h c) -> p h c", h=4)
        sgT = view(6304, 2080, "p (h c) -> p h c", h=4)
        vn = view(8384, 2580, "p (t h c) -> p t h c", t=NT, h=H)
        pst = view(10964, 1520)
        pp = view(12484, 1056, "p (b c) -> p b c", b=2)
        hn = view(13540, 1290, "p (b t c) -> p b t c", b=2, t=NT)
        Cs = [view(lo, 512, "p (h k) -> p h k", h=H) for lo in (14830, 16878)]
        qk_b = [view(lo + 512, 1024) for lo in (14830, 16878)]
        Cq_b = [x[:, 0:512].rearrange("p (h k) -> p h k", h=H) for x in qk_b]
        Ck_b = [x[:, 512:1024].rearrange("p (h k) -> p h k", h=H) for x in qk_b]
        tokz = view(15854, NE * R // 128)
        mixT = view(16878, 4160, "p (k c) -> p k c", k=KC)
        memn = view(16878, 2048, "p (m d) -> p m d", m=2)
        mkn = view(16878 + 2048, 2048, "p (m d) -> p m d", m=2)
        memT = view(2144, 2048, "p (k m) -> p k m", k=KC)
        irow, frow, brow, mrow, trow, zrow = [P[0:4, 16878 + 520 * i:16878 + 520 * (i + 1)] for i in range(6)]
        kw = gb[:, 0, 0:640].rearrange("p (t k) -> p t k", t=NT)
        Cout = gb[:, 1, 0:256]
        kvr = view(0, 6144, "p (s m d) -> p s m d", s=3, m=2)
        qcT = view(6304, 4160, "p (k c) -> p k c", k=KC)
        paT = view(10464, 4160, "p (h m c) -> p h m c", h=4, m=2)
        Er = view(14830, 1024, "p (s m) -> p s m", s=4)
        qb = view(15854, 1024)
        ctxT = mixT
        dnr = view(0, 6144, "p (s f d) -> p s f d", s=3, f=2)
        xg = view(6304, 3072, "p (s d) -> p s d", s=3)
        xgT = view(9376, 3072, "p (s k c) -> p s k c", s=3, k=KC)
        hh = view(12448, 768, "p (s f c) -> p s f c", s=3, f=2)
        sgm = view(13216, 512, "p (s f) -> p s f", s=2)
        ysb = view(13728, 3072, "p (s d) -> p s d", s=3)
        yg = view(16878, 4096, "p (s k d) -> p s k d", s=2, k=2)
        cache = smp[0:NS * NPOOL, 0:512]
        un = smp[:, 0:512]
        qsn, ksn, vsn, n0 = [smp[0:NS, 512 * i:512 * (i + 1)] for i in range(1, 5)]
        qs2 = smp[0:NS, 0:D]
        paz = smp[:, 0:2048].rearrange("p (m r c) -> p m r c", m=2, r=32)
        ctxs = smp[0:32, 2048:2304]
        Es = poolw[0:32, 0:2, :].rearrange("p a b -> p (a b)")
        sS = poolw[:, 2, 0:64].rearrange("p (m r) -> p m r", m=2)
        csum = sb("csum", [128, 4, NS])
        cq = sb("cq", [128, H, NS])
        vsT = sb("vsT", [128, H, NS])
        wcb = sb("wcb", [128, NS, H])
        mx4 = sb("mx4", [128, 12])
        rt = smp[0:TR, 0:NT * 100].rearrange("p (t c) -> p t c", t=NT)
        lgT = smp[0:20, 512:512 + 2 * TR].rearrange("p (b c) -> p b c", b=2)
        Mb16 = sb("Mb16", [TR, NT, NE], BF16)
        tok = sb("tok", [TR, NT], U32)
        dst = sb("dst", [TR, 2, NT], U32)
        idxl = sb("idxl", [C, NE], U32)
        idx1 = sb("idx1", [C, 1], U32)
        flag = sb("flag", [1, 1], I32)
        turn = sb("turn", [1, 2])

        act_full, act_free, dve_full, dve_free = sem("act_full"), sem("act_free"), sem("dve_full"), sem("dve_free")
        dve_step, act_step, pool_step = sem("dve_step"), sem("act_step"), sem("pool_step")
        mem_in, con_in, x_in, gb_in, small_in, cache_in = [sem(s) for s in ("mem_in", "con_in", "x_in", "gb_in", "small_in", "cache_in")]
        wgr_in, st_in, emb_in = sem("wgr_in"), sem("st_in"), sem("emb_in")
        blk_in = [sem(f"blk_in{i}") for i in range(WR)]
        x0_ready, x1_ready, x2_ready, x3_ready = sem("x0_ready"), sem("x1_ready"), sem("x2_ready"), sem("x3_ready")
        var_ready, rstd_ready = sem("var_ready"), sem("rstd_ready")
        out_done = sem("out_done")
        mk_out, mv_out = sem("mk_out"), sem("mv_out")
        memset_done = sem("memset_done")
        rows_act, rows_dve = sem("rows_act"), sem("rows_dve")
        mb_full, wexp_done, sel_done = sem("mb_full"), sem("wexp_done"), sem("sel_done")
        c_out, un_out, sn_out = sem("c_out"), sem("un_out"), sem("sn_out")
        sig_done = sem("sig_done")
        hn_ready, snat_ready = sem("hn_ready"), sem("snat_ready")
        sgate_dif, sgate_exp = sem("sgate_dif"), sem("sgate_exp")
        usum_done, dif_done = sem("usum_done"), sem("dif_done")
        bounce, cq_done, cupd_done = sem("bounce"), sem("cq_done"), sem("cupd_done")
        c_in = [sem(f"c_in{i}") for i in range(2)]
        c_store = [sem(f"c_store{i}") for i in range(2)]
        hs_var, hs_rstd, hs_ready = sem("hs_var"), sem("hs_rstd"), sem("hs_ready")
        sq2_out, kq_done = sem("sq2_out"), sem("kq_done")
        qb_in = [sem(f"qb_in{i}") for i in range(2)]
        kv_in = [sem(f"kv_in{i}") for i in range(3)]
        k_used, v_used = sem("k_used"), sem("v_used")
        nmax_done, prob_ready = sem("nmax_done"), sem("prob_ready")
        s_nmax, s_exp, s_prob, paz_zero = sem("s_nmax"), sem("s_exp"), sem("s_prob"), sem("paz_zero")
        x2_out = sem("x2_out")
        rt_act, rt_dve = sem("rt_act"), sem("rt_dve")
        mask_ready, dst_ready, lst_zero, lst_out, idx_in = [sem(s) for s in ("mask_ready", "dst_ready", "lst_zero", "lst_out", "idx_in")]
        xg_in = [sem(f"xg_in{i}") for i in range(3)]
        dn_in = [sem(f"dn_in{i}") for i in range(3)]
        xgT_full, xgT_act, xgT_dve = sem("xgT_full"), sem("xgT_act"), sem("xgT_dve")
        gu_full, sgm_ready, hh_ready, y_full = sem("gu_full"), sem("sgm_ready"), sem("hh_ready"), sem("y_full")
        y_act, y_dve = sem("y_act"), sem("y_dve")
        y_out = [sem(f"y_out{i}") for i in range(3)]
        flag_ready, ov_turn = sem("flag_ready"), sem("ov_turn")
        hsteps, ovs = sem("hsteps"), sem("ovs")
        yg_in = [sem(f"yg_in{i}") for i in range(2)]
        yg_used, xa_ready = sem("yg_used"), sem("xa_ready")
        ov_w, ov_idx, ov_x, ov_t, ov_tc, ov_gu, ov_sg, ov_h, ov_y, ov_yc, ov_out = [sem(s) for s in (
            "ov_w", "ov_idx", "ov_x", "ov_t", "ov_tc", "ov_gu", "ov_sg", "ov_h", "ov_y", "ov_yc", "ov_out")]

        block = ctx.enter_context(nc.Block())

        at, used = {}, {}

        def wcols(w, c0, n=512):
            return w[0].rearrange("(k p) c -> p k c", p=128)[:, :, c0:c0 + n]

        BLOCKS = [("wk0", wcols(a["ca_wk"], 0)), ("wk1", wcols(a["ca_wk"], 512)),
                  ("wv0", wcols(a["ca_wv"], 0)), ("wv1", wcols(a["ca_wv"], 512)),
                  ("q", wcols(a["w_in"], PW)), ("k", wcols(a["w_in"], PW + 512)),
                  ("v", wcols(a["w_in"], PW + 1024)), ("og", wcols(a["w_in"], PW + 1536)),
                  ("u", wcols(a["w_in"], 0)),
                  ("wo0", wcols(a["w_out"], 0)), ("wo1", wcols(a["w_out"], 512)),
                  ("wq0", wcols(a["ca_wq"], 0)), ("wq1", wcols(a["ca_wq"], 512)),
                  ("wc0", wcols(a["ca_wo"], 0)), ("wc1", wcols(a["ca_wo"], 512))]
        BI = {name: i for i, (name, _) in enumerate(BLOCKS)}
        NB = len(BLOCKS)
        assert NB % WR == 0
        gate_w = a["w_gate"][0].rearrange("e (k p) f -> p e k f", p=128)
        up_w = a["w_up"][0].rearrange("e (k p) f -> p e k f", p=128)
        down_w = a["w_down"][0].rearrange("e (f p) d -> p e f d", p=128)
        one_expert = lambda w, e: w[:, bass.ds(e, 1)].rearrange("p one k f -> p (one k) f")
        kv_src = [a["cache_mem_k"][0, b] for b in range(NS)] + [a["cache_mem_v"][0, b] for b in range(NS)]

        @block.tensor
        def _(pe):
            na, nd = [0], [0]

            def bank_a():
                k = na[0]
                na[0] += 1
                if k >= 3:
                    pe.wait_ge(act_free, k - 2)
                return RING_A[k % 3]

            def bank_d():
                k = nd[0]
                nd[0] += 1
                if k >= 3:
                    pe.wait_ge(dve_free, k - 2)
                return RING_D[k % 3]

            mm = nc.tensor.matmul

            def use_block(name):
                i = BI[name]
                pe.wait_ge(blk_in[i % WR], 16 * (i // WR + 1))
                return wring[:, i % WR]

            def contract(out, lhs, rhs, n=KC):
                for k in range(n):
                    last = mm(out, lhs(k), rhs(k), start=(k == 0), stop=(k == n - 1))
                return last

            def project(name, cts, src=xT, groups=GRP):
                w = use_block(name)
                for ct in cts:
                    for c0, cn in groups:
                        bk = bank_a()
                        last = contract(bk[:, 0:cn], lambda k: w[:, k, ct * 128:ct * 128 + 128],
                                        lambda k: src[:, k, c0:c0 + cn])
                        last.then_inc(act_full, 1)
                used[BI[name]] = (act_full, na[0])

            pe.wait_ge(con_in, 16)
            pe.wait_ge(mem_in, 16)
            for m in range(2):
                for q in range(2):
                    bk = bank_a()
                    for k in range(4):
                        last = nc.tensor.transpose(bk[:, k * 128:k * 128 + 128], memn[:, m, (4 * q + k) * 128:(4 * q + k + 1) * 128], ident)
                    last.then_inc(act_full, 1)
            pe.wait_ge(act_free, 4)
            for name in ("wk0", "wk1", "wv0", "wv1"):
                w = use_block(name)
                for m in range(2):
                    bk = bank_a()
                    last = contract(bk[:, :], lambda k: memT[:, k, m * 128:m * 128 + 128], lambda k: w[:, k, :])
                    last.then_inc(act_full, 1)
                used[BI[name]] = (act_full, na[0])
            pe.wait_ge(cache_in, 16)
            bk = bank_d()
            n = NS * NPOOL
            for g in range(4):
                last = nc.tensor.transpose(bk[:, g * n:g * n + n], cache[:, g * 128:g * 128 + 128], ident[0:n, 0:n])
            last.then_inc(dve_full, 1)
            pe.wait_ge(act_free, 8)
            for m in range(2):
                for q in range(2):
                    bk = bank_a()
                    for k in range(4):
                        last = nc.tensor.transpose(bk[:, k * 128:k * 128 + 128], mkn[:, m, (4 * q + k) * 128:(4 * q + k + 1) * 128], ident)
                    last.then_inc(act_full, 1)

            def transpose_x(t, ready):
                pe.wait_ge(ready, t + 1)
                for q in range(2):
                    bk = bank_a()
                    for k in range(4):
                        last = nc.tensor.transpose(bk[:, k * TR:k * TR + TR], xn[0:TR, t, (4 * q + k) * 128:(4 * q + k + 1) * 128], ident[0:TR, 0:TR])
                    last.then_inc(act_full, 1)

            for t in range(NT):
                transpose_x(t, x0_ready)
            pe.wait_ge(act_free, na[0])
            pe.wait_ge(wgr_in, 64)
            for c0, cn in GRP:
                bk = bank_a()
                contract(bk[0:36, 0:cn], lambda k: wg[:, k, :], lambda k: xT[:, k, c0:c0 + cn]).then_inc(act_full, 1)
            project("q", range(4))
            project("k", range(4))
            qk_groups = na[0]
            w = use_block("v")
            for t in range(NT):
                bk = bank_d()
                contract(bk[0:TR, :], lambda k: xT[:, k, t * TR:t * TR + TR], lambda k: w[:, k, :]).then_inc(dve_full, 1)
            used[BI["v"]] = (dve_full, nd[0])
            at["values"] = nd[0]
            pe.wait_ge(rows_act, 2)
            pe.wait_ge(rows_dve, 2)
            bk = bank_d()
            for t in range(NT):
                r = rows_of(t)
                nc.tensor.transpose(bk[0:r, 4 * t:4 * t + 4], irow[:, t * TR:t * TR + r], ident[0:4, 0:4])
                nc.tensor.transpose(bk[0:r, 20 + 4 * t:24 + 4 * t], trow[:, t * TR:t * TR + r], ident[0:4, 0:4])
            nc.tensor.transpose(bk[0:NS, 40:44], irow[:, NP_:NTOK], ident[0:4, 0:4])
            nc.tensor.transpose(bk[0:NS, 44:48], frow[:, NP_:NTOK], ident[0:4, 0:4]).then_inc(dve_full, 1)
            at["gcol"] = nd[0]
            pe.wait_ge(act_free, qk_groups)
            for src in (qT, kT):
                bk = bank_d()
                for h in range(H):
                    last = nc.tensor.transpose(bk[0:NS, h * 128:h * 128 + 128], src[:, h, NP_:NTOK], ident)
                last.then_inc(dve_full, 1)
            pe.wait_ge(dve_free, at["values"])
            bk = bank_d()
            for h in range(H):
                last = nc.tensor.transpose(bk[:, h * NS:h * NS + NS], vsn[:, h * 128:h * 128 + 128], ident[0:NS, 0:NS])
            last.then_inc(dve_full, 1)

            offs = [0]
            for t in range(NT):
                offs.append(offs[-1] + NP_ - t * TR)

            def scores(h):
                if h >= 2:
                    pe.wait_ge(wexp_done, NT * (h - 1))
                mm(MBANK[h % 2][:, :], ident[0:4, h:h + 1].broadcast_to([4, 128]), mrow[:, 0:NP_], start=True, stop=True).then_inc(mb_full, 1)
                for t in range(NT):
                    r = rows_of(t)
                    bk = bank_d()
                    mm(bk[0:r, 0:NP_ - t * TR], kT[:, h, t * TR:t * TR + r], qT[:, h, t * TR:NP_], start=True, stop=True).then_inc(dve_full, 1)
                    at["scores", h, t] = nd[0]
                bk = bank_d()
                for t in range(4):
                    last = nc.tensor.transpose(bk[0:TR, t * 128:t * 128 + 128], kT[:, h, t * TR:t * TR + TR], ident)
                last.then_inc(dve_full, 1)
                bk = bank_d()
                nc.tensor.transpose(bk[0:LAST, 0:128], kT[:, h, 4 * TR:NP_], ident).then_inc(dve_full, 1)
                at["keys", h] = nd[0]

            def numerators(h):
                for j in range(NT):
                    pe.wait_ge(sel_done, NT * h + j + 1)
                    bk = bank_a()
                    nj = rows_of(j)
                    for i in range(j + 1):
                        ni = rows_of(i)
                        c0 = offs[i] + (j - i) * TR
                        last = mm(bk[0:nj, 0:HD + 1], pst[0:ni, c0:c0 + nj], vn[0:ni, i, h, :], start=(i == 0), stop=(i == j))
                    last.then_inc(act_full, 1)
                at["numerators", h] = na[0]

            def state(h):
                pe.wait_ge(dve_free, at["keys", h])
                bk = bank_d()
                for i in range(NT):
                    ni = rows_of(i)
                    mm(bk[:, 0:HD], vn[0:ni, i, h, 0:HD], kw[0:ni, i, :], start=(i == 0), stop=(i == NT - 1))
                for i in range(NT):
                    ni = rows_of(i)
                    last = mm(bk[0:1, HD:2 * HD], vn[0:ni, i, h, HD:HD + 1], kw[0:ni, i, :], start=(i == 0), stop=(i == NT - 1))
                last.then_inc(dve_full, 1)
                at["state", h] = nd[0]

            def transpose_heads(h):
                pe.wait_ge(hn_ready, h + 1)
                bk = bank_d()
                for t in range(NT):
                    r = rows_of(t)
                    last = nc.tensor.transpose(bk[:, t * TR:t * TR + r], hn[0:r, h % 2, t, 0:HD], ident[0:r, 0:r])
                last.then_inc(dve_full, 1)
                at["heads", h] = nd[0]

            def transpose_last(i):
                pe.wait_ge(act_free, at["u", i])
                bk = bank_d()
                for g in range(2):
                    last = nc.tensor.transpose(bk[0:NPOOL + NS, g * 128:g * 128 + 128], uT[:, 2 * i + g, PADC + NP_ - NPOOL:PADC + NTOK], ident)
                last.then_inc(dve_full, 1)
                at["last u", i] = nd[0]

            pe.wait_ge(memset_done, 1)
            scores(0)
            project("og", (0, 1))
            at["og", 0] = na[0]
            numerators(0)
            state(0)
            scores(1)
            project("og", (2, 3))
            at["og", 1] = na[0]
            transpose_heads(0)
            numerators(1)
            state(1)
            scores(2)
            project("u", (0, 1))
            at["u", 0] = na[0]
            transpose_heads(1)
            transpose_last(0)
            numerators(2)
            state(2)
            scores(3)
            project("u", (2, 3))
            at["u", 1] = na[0]
            transpose_heads(2)
            transpose_last(1)
            numerators(3)
            state(3)
            for g in range(4):
                pe.wait_ge(dif_done, g + 1)
                for c0, cn in GRP:
                    bk = bank_a()
                    mm(bk[:, 0:cn], poolw[:, g, :], uT[:, g, PADC + c0:PADC + c0 + cn], start=True, stop=True).then_inc(act_full, 1)
            at["pool"] = na[0]
            transpose_heads(3)

            def rows_project(t, names, src):
                for name in names:
                    w = use_block(name)
                    bk = bank_d()
                    contract(bk[0:TR, :], lambda k: src[:, k, t * TR:t * TR + TR], lambda k: w[:, k, :]).then_inc(dve_full, 1)
                    used[BI[name]] = (dve_full, nd[0])

            WO = ("wo0", "wo1")
            pe.wait_ge(act_free, na[0])
            pe.wait_ge(dve_free, nd[0])
            rows_project(0, WO, mixT)
            rows_project(1, WO, mixT)
            transpose_x(0, x1_ready)
            pe.wait_ge(cq_done, NS)
            bk = bank_d()
            for h in range(H):
                last = nc.tensor.transpose(bk[0:NS, h * 128:h * 128 + 128], cq[:, h, :], ident)
            last.then_inc(dve_full, 1)
            rows_project(2, WO, mixT)
            transpose_x(1, x1_ready)
            pe.wait_ge(hs_ready, 1)
            bk = bank_d()
            for h in range(H):
                last = nc.tensor.transpose(bk[:, h * NS:h * NS + NS], vsn[:, h * 128:h * 128 + 128], ident[0:NS, 0:NS])
            last.then_inc(dve_full, 1)
            samples_mixed = nd[0]
            rows_project(3, WO, mixT)
            transpose_x(2, x1_ready)
            pe.wait_ge(dve_free, samples_mixed)
            rows_project(4, WO, mixT)
            transpose_x(3, x1_ready)

            project("wq0", range(4), groups=GRP[0:1])
            transpose_x(4, x1_ready)
            pe.wait_ge(act_free, na[0])
            project("wq0", range(4), groups=GRP[1:2])
            project("wq1", range(4), groups=GRP[1:2])
            pe.wait_ge(act_free, na[0])
            for q in range(2):
                bk = bank_a()
                for k in range(4):
                    last = nc.tensor.transpose(bk[0:NS, k * 128:k * 128 + 128], qcT[:, 4 * q + k, NP_:NTOK], ident)
                last.then_inc(act_full, 1)
            at["sample q"] = na[0]
            project("wq1", range(4), groups=GRP[0:1])
            pe.wait_ge(act_free, na[0])

            NQ = NT * 4

            def attend(n):
                t, h = divmod(n, 4)
                bk = bank_a()
                for k in range(2):
                    last = mm(bk[0:TR, 0:NM], qcT[:, 2 * h + k, t * TR:t * TR + TR], mkT[:, 2 * h + k, :], start=(k == 0), stop=(k == 1))
                last.then_inc(act_full, 1)
                at["attend", n] = na[0]

            def transpose_probs(n):
                pe.wait_ge(prob_ready, n + 1)
                bk = bank_a()
                for m in range(2):
                    last = nc.tensor.transpose(bk[:, m * TR:m * TR + TR], Er[0:TR, n % 4, m * 128:m * 128 + 128], ident[0:TR, 0:TR])
                last.then_inc(act_full, 1)
                at["probs", n] = na[0]

            def context(h, ec, group):
                c0, cn = group
                bk = bank_a()
                for m in range(2):
                    last = mm(bk[:, 0:cn], mv[:, m, h * CE + ec * 128:h * CE + ec * 128 + 128], paT[:, h, m, c0:c0 + cn], start=(m == 0), stop=(m == 1))
                last.then_inc(act_full, 1)

            for n in range(NQ):
                attend(n)
                if n >= 3:
                    transpose_probs(n - 3)
                if n >= 16:
                    pe.wait_ge(act_free, at["probs", 11])
                    for g in (2 * (n - 16), 2 * (n - 16) + 1):
                        context(g // 2, g % 2, GRP[0])
            for n in range(NQ - 3, NQ):
                transpose_probs(n)
            pe.wait_ge(k_used, NS)
            bk = bank_d()
            for m in range(2):
                last = nc.tensor.transpose(bk[0:32, m * 128:m * 128 + 128], sS[:, m, :], ident)
            last.then_inc(dve_full, 1)
            at["sample scores"] = nd[0]
            pe.wait_ge(act_free, at["probs", NQ - 1])
            for g in range(8):
                context(g // 2, g % 2, GRP[1])
            pe.wait_ge(s_prob, 1)
            bk = bank_d()
            for m in range(2):
                last = nc.tensor.transpose(bk[:, m * 32:m * 32 + 32], Es[:, m * 128:m * 128 + 128], ident[0:32, 0:32])
            last.then_inc(dve_full, 1)
            pe.wait_ge(dve_free, nd[0])
            bk = bank_d()
            for b in range(NS):
                n = NS + b
                pe.wait_ge(kv_in[n % 3], 16 * (n // 3 + 1))
                for h in range(4):
                    for m in range(2):
                        last = mm(bk[0:32, 0:CE], paz[:, m, 4 * b + h, :], kvr[:, n % 3, m, h * CE:h * CE + CE],
                                  start=(b + h + m == 0), stop=(b == NS - 1 and h == 3 and m == 1))
                if b < NS - 1:
                    last.then_inc(v_used, 1)
            last.then_inc(dve_full, 1)
            at["sample context"] = nd[0]
            pe.wait_ge(dve_free, nd[0])
            bk = bank_d()
            for ec in range(2):
                last = nc.tensor.transpose(bk[:, ec * 32:ec * 32 + 32], ctxs[:, ec * 128:ec * 128 + 128], ident[0:32, 0:32])
            last.then_inc(dve_full, 1)

            def router(t):
                bk = bank_a()
                contract(bk[0:20, 0:TR], lambda k: wr[:, k, :], lambda k: xT[:, k, t * TR:t * TR + TR]).then_inc(act_full, 1)
                at["router", t] = na[0]

            def router_rows(t):
                pe.wait_ge(act_free, at["router", t])
                bk = bank_d()
                nc.tensor.transpose(bk[0:TR, 0:20], lgT[:, t % 2, :], ident[0:20, 0:20]).then_inc(dve_full, 1)
                at["router rows", t] = nd[0]

            pe.wait_ge(act_free, na[0])
            pe.wait_ge(dve_free, nd[0])
            WC = ("wc0", "wc1")
            for t in range(NT):
                rows_project(t, WC, ctxT)
                if t >= 1:
                    transpose_x(t - 1, x2_ready)
                    pe.wait_ge(act_free, na[0])
                    router(t - 1)
                if t >= 2:
                    router_rows(t - 2)
            router_rows(NT - 2)
            transpose_x(NT - 1, x2_ready)
            pe.wait_ge(act_free, na[0])
            router(NT - 1)
            router_rows(NT - 1)
            pe.wait_ge(mask_ready, 1)
            bk = bank_d()
            for t in range(NT + 1):
                for i in range(min(t + 1, NT)):
                    last = mm(bk[0:TR, t * NE:t * NE + NE], (trib if i == t else onesb)[:, :], Mb16[:, i, :],
                              start=(i == 0), stop=(i == min(t, NT - 1)))
            last.then_inc(dve_full, 1)

            pe.wait_ge(dve_free, nd[0])

            GU = [ps[2], ps[3], ps[6]]
            YB = [ps[4], ps[5]]

            def turn_rows(e, s, k):
                if not (isinstance(e, int) and e == 0):
                    pe.wait_ge(xgT_act, e)
                    pe.wait_ge(xgT_dve, e)
                pe.wait_ge(xg_in[s], k * 16 + 16)
                for q in range(2):
                    for j in range(4):
                        kk = 4 * q + j
                        last = nc.tensor.transpose(ps[q][:, j * C:j * C + C], xg[:, s, kk * 128:kk * 128 + 128], ident)
                    last.then_inc(xgT_full, 1)

            def gate_up(e, s, k):
                pe.wait_ge(blk_in[s], k * 32 + (16 * (NB // WR) + 32))
                pe.wait_ge(xgT_act, e + 1)
                pe.wait_ge(xgT_dve, e + 1)
                for f in range(4):
                    last = contract(GU[s][:, f * C:f * C + C], lambda kk: wring[:, s, kk, f * 128:f * 128 + 128],
                                    lambda kk: xgT[:, s, kk, :])
                last.then_inc(gu_full, 1)

            def down(e, s, k, first=False):
                pe.wait_ge(dn_in[s], k * 16 + 16)
                pe.wait_ge(hh_ready, e + 1)
                if not first:
                    pe.wait_ge(y_act, e)
                    pe.wait_ge(y_dve, e)
                for q in range(2):
                    for f in range(2):
                        last = mm(YB[q][:, :], hh[:, s, f, :], dnr[:, s, f, q * 512:q * 512 + 512], start=(f == 0), stop=(f == 1))
                last.then_inc(y_full, 1)

            turn_rows(0, 0, 0)
            gate_up(0, 0, 0)
            turn_rows(1, 1, 0)
            gate_up(1, 1, 0)
            turn_rows(2, 2, 0)
            down(0, 0, 0, first=True)

            def expert_step(e, u, i):
                nxt, prv = (u + 1) % 3, (u + 2) % 3
                gate_up(e, u, i)
                turn_rows(e + 1, nxt, i + (1 if u == 2 else 0))
                down(e - 1, prv, i - (1 if u == 0 else 0))

            for e in (2, 3):
                expert_step(e, e % 3, e // 3)
            with pe.Fori(1, 4) as i:
                for u in range(1, 4):
                    expert_step(i * 3 + u, u % 3, i + u // 3)
            for e in (13, 14):
                expert_step(e, e % 3, e // 3)
            gate_up(15, 0, 5)
            down(14, 2, 4)
            down(15, 0, 5)

            pe.wait_ge(flag_ready, 1)
            over = pe.value_load(flag[0:1, 0:1], min_val=0, max_val=1)
            with pe.If(over > 0):
                with pe.Fori(0, NE) as e:
                    pe.wait_ge(ov_w, e * 48 + 48)
                    for c in range(1, NCH):
                        n = e * (NCH - 1) + (c - 1)
                        pe.wait_ge(ov_x, n * 16 + 16)
                        for q in range(2):
                            for j in range(4):
                                kk = 4 * q + j
                                last = nc.tensor.transpose(ps[q][:, j * C:j * C + C], xg[:, 0, kk * 128:kk * 128 + 128], ident)
                        last.then_inc(ov_t, 1)
                        pe.wait_ge(ov_tc, n + 1)
                        for f in range(4):
                            last = contract(GU[0][:, f * C:f * C + C], lambda kk: wring[:, 0, kk, f * 128:f * 128 + 128],
                                            lambda kk: xgT[:, 0, kk, :])
                        last.then_inc(ov_gu, 1)
                        pe.wait_ge(ov_h, n + 1)
                        for q in range(2):
                            for f in range(2):
                                last = mm(YB[q][:, :], hh[:, 0, f, :], dnr[:, 0, f, q * 512:q * 512 + 512], start=(f == 0), stop=(f == 1))
                        last.then_inc(ov_y, 1)

        @block.sync
        def _(sp):
            def block_load(i):
                if i >= WR:
                    sp.wait_ge(*used[i - WR])
                sp.dma_start(wring[:, i % WR], BLOCKS[i][1]).then_inc(blk_in[i % WR], 16)

            def kv_load(n):
                if n >= 3:
                    if n - 3 < NS:
                        sp.wait_ge(k_used, n - 2)
                    else:
                        sp.wait_ge(v_used, n - 3 - NS + 1)
                sp.dma_start(kvr[:, n % 3], kv_src[n].rearrange("(m p) h e -> p m (h e)", p=128)).then_inc(kv_in[n % 3], 16)

            def expert_load(e, s):
                sp.dma_start(wring[:, s, :, 0:DE], one_expert(gate_w, e)).then_inc(blk_in[s], 16)
                sp.dma_start(wring[:, s, :, DE:2 * DE], one_expert(up_w, e)).then_inc(blk_in[s], 16)

            def down_load(e, s):
                sp.dma_start(dnr[:, s], one_expert(down_w, e)).then_inc(dn_in[s], 16)

            sp.dma_start(memn, a["mem_prompt"][0].rearrange("(m p) d -> p m d", p=128)).then_inc(mem_in, 16)
            for i in range(BI["wc0"] + 1):
                block_load(i)
            sp.wait_ge(act_full, at["pool"])
            for n in range(3):
                kv_load(n)
            block_load(BI["wc1"])
            sp.wait_ge(sq2_out, 16)
            for i in range(2):
                sp.wait_ge(c_store[i], 16 * NS // 2)
            for b in range(NS):
                for hf in range(2):
                    if b >= 1:
                        sp.wait_ge(kq_done, 2 * (b - 1) + hf + 1)
                    sp.dma_start(qb[:, hf * 512:hf * 512 + 512], sq2_d[b, hf * 512:hf * 512 + 512].partition_broadcast(128)).then_inc(qb_in[hf], 16)
                if b >= 1:
                    kv_load(b + 2)
            sp.wait_ge(*used[NB - WR])
            expert_load(0, 0)
            for n in range(NS + 2, 2 * NS):
                kv_load(n)
            sp.wait_ge(dve_full, at["sample context"])
            for e in range(3):
                down_load(e, e)
            for e in (1, 2):
                sp.wait_ge(*used[NB - WR + e])
                expert_load(e, e)

            def refill(e, s):
                sp.wait_ge(gu_full, e - 2)
                expert_load(e, s)
                sp.wait_ge(y_full, e - 2)
                down_load(e, s)

            with sp.Fori(0, 4) as i:
                for u in range(3):
                    refill(i * 3 + (3 + u), u)
            refill(NE - 1, (NE - 1) % 3)

            sp.wait_ge(flag_ready, 1)
            over = sp.value_load(flag[0:1, 0:1], min_val=0, max_val=1)
            with sp.If(over > 0):
                sp.wait_ge(gu_full, NE)
                sp.wait_ge(lst_out, 16 * 2 * NT)
                sp.wait_ge(y_full, NE)
                with sp.Fori(0, NE) as e:
                    sp.dma_start(wring[:, 0, :, 0:DE], one_expert(gate_w, e)).then_inc(ov_w, 16)
                    sp.dma_start(wring[:, 0, :, DE:2 * DE], one_expert(up_w, e)).then_inc(ov_w, 16)
                    sp.dma_start(dnr[:, 0], one_expert(down_w, e)).then_inc(ov_w, 16)
                    for c in range(1, NCH):
                        n = e * (NCH - 1) + (c - 1)
                        sp.dma_start(idx1[:, :], lst_e[c * C:c * C + C, bass.ds(e, 1)], allow_slow_non_contiguous=True).then_inc(ov_idx, 16)
                        sp.wait_ge(ov_turn, n + 1)
                        sp.wait_ge(ov_yc, n + 1)
                        sp.dma_start(y_e[c * C:c * C + C, bass.ds(e, 1), :], ysb[:, 0:1]).then_inc(ov_out, 16)
            sp.wait_ge(out_done, 16 * (2 + NT + 1))
            for i in range(2):
                sp.wait_ge(c_store[i], 16 * NS // 2)
            sp.wait_ge(c_out, 32 * H)
            sp.wait_ge(mk_out, 64)
            sp.wait_ge(mv_out, 64)
            sp.wait_ge(un_out, 48)
            sp.wait_ge(sn_out, 16)

        @block.scalar
        def _(act):
            nf = [0]
            steps = [0]
            A = nc.scalar.activation

            def full():
                k = nf[0]
                nf[0] += 1
                act.wait_ge(act_full, k + 1)
                return RING_A[k % 3]

            def link(ins):
                steps[0] += 1
                ins.then_inc(act_step, 1)
                act.wait_ge(act_step, steps[0])

            act.dma_start(con[:, :], a["consts"]).then_inc(con_in, 16)
            xp = a["x_prompt"][0]
            for t in range(NT):
                act.dma_start(xn[0:rows_of(t), t, :], xp[t * TR:t * TR + rows_of(t), :]).then_inc(x_in, 16)
            act.dma_start(xn[LAST:TR, NT - 1, :], a["x_sample"][:, 0, :]).then_inc(x_in, 16)
            act.dma_start(gb[:, 0, :], a["emb_ln_g"].partition_broadcast(128)).then_inc(emb_in, 16)
            act.dma_start(gb[:, 1, :], a["emb_ln_b"].partition_broadcast(128)).then_inc(emb_in, 16)
            act.dma_start(cache, a["cache_pool"][0].rearrange("b r c -> (b r) c")).then_inc(cache_in, 16)

            for m in range(2):
                for q in range(2):
                    bk = full()
                    A(memT[:, 4 * q:4 * q + 4, m * 128:m * 128 + 128], bk[:, :].rearrange("p (k c) -> p k c", k=4), ACT.Copy).then_inc(act_free, 1)
            for name, dstn in (("k", mkn), ("v", mv)):
                for hf in range(2):
                    for m in range(2):
                        bk = full()
                        A(dstn[:, m, hf * 512:hf * 512 + 512], bk[:, :], ACT.Copy).then_inc(act_free, 1)
                        act.wait_ge(act_free, nf[0])
                        out = (o_pmk if name == "k" else o_pmv)[0, 0].rearrange("(m p) h e -> p m (h e)", p=128)
                        act.dma_start(out[:, m, hf * 512:hf * 512 + 512], dstn[:, m, hf * 512:hf * 512 + 512]).then_inc(mk_out if name == "k" else mv_out, 16)
            for m in range(2):
                for q in range(2):
                    bk = full()
                    A(mkT[:, 4 * q:4 * q + 4, m * 128:m * 128 + 128], bk[:, :].rearrange("p (k c) -> p k c", k=4), ACT.Copy).then_inc(act_free, 1)

            def take_x(t):
                for q in range(2):
                    bk = full()
                    A(xT[:, 4 * q:4 * q + 4, t * TR:t * TR + TR], bk[:, 0:4 * TR].rearrange("p (k c) -> p k c", k=4), ACT.Copy).then_inc(act_free, 1)

            for t in range(NT):
                take_x(t)
            act.wait_ge(small_in, 16 * 13)
            act.wait_ge(mk_out, 64)
            for c0, cn in GRP:
                bk = full()
                A(irow[:, c0:c0 + cn], bk[0:4, 0:cn], ACT.Identity, bias=colv[0:4, 8:9])
                A(frow[:, c0:c0 + cn], bk[32:36, 0:cn], ACT.Identity, bias=colv[32:36, 9:10]).then_inc(act_free, 1)
            act.wait_ge(act_free, nf[0])
            link(A(trow, frow, ACT.Abs))
            link(A(trow, trow, ACT.Exp, scale=-1.0))
            A(trow, trow, ACT.Ln, bias=1.0).then_inc(rows_act, 1)

            def take_projection(dstn, cts, scale, groups=GRP, off=0):
                for ct in cts:
                    for c0, cn in groups:
                        bk = full()
                        A(dstn[:, ct, off + c0:off + c0 + cn], bk[:, 0:cn], ACT.Copy, scale=scale).then_inc(act_free, 1)

            take_projection(qT, range(4), HD ** -0.5)
            act.wait_ge(rows_dve, 1)
            A(trow[:, 0:NP_], trow[:, 0:NP_], ACT.Exp, scale=-1.0).then_inc(rows_act, 1)
            take_projection(kT, range(4), 1.0)

            offs = [0]
            for t in range(NT):
                offs.append(offs[-1] + NP_ - t * TR)

            def weights(h):
                act.wait_ge(mb_full, h + 1)
                mb = MBANK[h % 2]
                act.wait_ge(dve_free, at["gcol"])
                for t in range(NT):
                    r = rows_of(t)
                    bias = gcol[0:r, 4 * t + h:4 * t + h + 1]
                    A(wcol[0:r, t, h:h + 1], mb[0:r, NP_ - 1:NP_], ACT.Exp, bias=bias)
                    ins = A(pst[0:r, offs[t]:offs[t + 1]], mb[0:r, t * TR:NP_], ACT.Exp, bias=bias)
                    ins.then_inc(wexp_done, 1)

            def take_numerators(h):
                if h >= 2:
                    act.wait_ge(dve_full, at["heads", h - 2])
                for j in range(NT):
                    bk = full()
                    r = rows_of(j)
                    A(hn[0:r, h % 2, j, :], bk[0:r, 0:HD + 1], ACT.Copy).then_inc(act_free, 1)

            def take_og(cts):
                for ct in cts:
                    for c0, cn in GRP:
                        bk = full()
                        A(sgT[:, ct, c0:c0 + cn], bk[:, 0:cn], ACT.Exp, scale=-1.0).then_inc(act_free, 1)
                act.wait_ge(act_free, nf[0])
                x = sgT[:, cts[0]:cts[1] + 1, :]
                link(A(x, x, ACT.Ln, bias=1.0))
                A(x, x, ACT.Exp, scale=-1.0).then_inc(sig_done, 1)

            weights(0)
            act.wait_ge(sgate_dif, 1)
            A(sg8[:, 12:20], sg8[:, 12:20], ACT.Exp)
            A(sg8[:, 20:24], sg8[:, 8:12], ACT.Exp, scale=-1.0).then_inc(sgate_exp, 1)
            take_og((0, 1))
            take_numerators(0)
            weights(1)
            take_og((2, 3))
            take_numerators(1)
            weights(2)
            take_projection(uT, (0, 1), 1.0, off=PADC)
            take_numerators(2)
            weights(3)
            take_projection(uT, (2, 3), 1.0, off=PADC)
            take_numerators(3)
            for i in range(2):
                act.wait_ge(c_store[i], 16 * NS // 2)
            for g in range(4):
                for c0, cn in GRP:
                    bk = full()
                    A(mixT[:, g, c0:c0 + cn], bk[:, 0:cn], ACT.Copy, scale=colv[:, g:g + 1]).then_inc(act_free, 1)
            for t in range(4):
                take_x(t)
            def take_queries(b, groups):
                take_projection(qcT[:, 4 * b:4 * b + 4, :], range(4), CE ** -0.5, groups=groups)

            take_queries(0, GRP[0:1])
            take_x(4)
            take_queries(0, GRP[1:2])
            take_queries(1, GRP[1:2])
            act.wait_ge(un_out, 48)
            for q in range(2):
                bk = full()
                A(qs2[:, q * 512:q * 512 + 512], bk[0:NS, :], ACT.Copy).then_inc(act_free, 1)
            take_queries(1, GRP[0:1])

            def take_context(h, ec, group, samples):
                c0, cn = group
                bk = full()
                cn -= samples
                A(ctxT[:, 2 * h + ec, c0:c0 + cn], bk[:, 0:cn], ACT.Copy).then_inc(act_free, 1)

            def take_probs(n):
                t, h = divmod(n, 4)
                bk = full()
                A(paT[:, h, :, t * TR:t * TR + TR], bk[:, 0:2 * TR].rearrange("p (m c) -> p m c", m=2), ACT.Copy).then_inc(act_free, 1)

            NQ = NT * 4
            for n in range(NQ):
                bk = full()
                act.wait_ge(nmax_done, n + 1)
                A(Er[0:TR, n % 4, :], bk[0:TR, 0:NM], ACT.Exp, bias=mx4[0:TR, n % 4:n % 4 + 1], accum_out=mx4[0:TR, 4 + n % 4:5 + n % 4]).then_inc(act_free, 1)
                if n >= 3:
                    take_probs(n - 3)
                if n >= 16:
                    for g in (2 * (n - 16), 2 * (n - 16) + 1):
                        take_context(g // 2, g % 2, GRP[0], 0)
            for n in range(NQ - 3, NQ):
                take_probs(n)
            for g in range(4):
                take_context(g // 2, g % 2, GRP[1], NS)
            act.wait_ge(s_nmax, 1)
            A(Es, RING_D[(at["sample scores"] - 1) % 3][0:32, 0:NM], ACT.Exp, bias=mx4[0:32, 0:1], accum_out=mx4[0:32, 4:5]).then_inc(s_exp, 1)
            for g in range(4, 8):
                take_context(g // 2, g % 2, GRP[1], NS)

            def take_router(t):
                bk = full()
                if t >= 2:
                    act.wait_ge(dve_full, at["router rows", t - 2])
                A(lgT[:, t % 2, :], bk[0:20, 0:TR], ACT.Identity, bias=colv[0:20, 10:11]).then_inc(act_free, 1)

            for t in range(NT):
                take_x(t)
                take_router(t)
            act.wait_ge(rt_dve, 1)
            A(rt[:, :, 20:24], rt[:, :, 20:24], ACT.Exp).then_inc(rt_act, 1)
            act.wait_ge(rt_dve, 2)
            A(rt[:, :, 93:94], rt[:, :, 93:94], ACT.Exp).then_inc(rt_act, 1)
            act.wait_ge(x2_out, 16 * NT)
            for t in range(NT):
                A(xn[0:TR, t, :], xn[0:TR, t, :], ACT.Copy, scale=ALPHA).then_inc(xa_ready, 1)

            GU = [ps[2], ps[3], ps[6]]

            def expert_in(e, s):
                act.wait_ge(xgT_full, e * 2 + 1)
                A(xgT[:, s, 0:4, :], ps[0][:, :].rearrange("p (k c) -> p k c", k=4), ACT.Copy).then_inc(xgT_act, 1)

            def expert_exp(e, s):
                act.wait_ge(gu_full, e + 1)
                if not (isinstance(e, int) and e < 1):
                    act.wait_ge(hh_ready, e)
                A(sgm[:, 0, :], GU[s][:, 0:2 * C], ACT.Exp, scale=-1.0).then_inc(sgm_ready, 1)

            def expert_out(e, s, k):
                act.wait_ge(y_full, e + 1)
                if not (isinstance(k, int) and k == 0):
                    act.wait_ge(y_out[s], k * 16)
                A(ysb[:, s, 0:512], ps[4][:, :], ACT.Copy).then_inc(y_act, 1)
                act.wait_ge(y_act, e + 1)
                act.wait_ge(y_dve, e + 1)
                act.dma_start(y_e[0:C, bass.ds(e, 1), :], ysb[:, s:s + 1]).then_inc(y_out[s], 16)

            expert_in(0, 0)
            expert_exp(0, 0)
            expert_in(1, 1)
            expert_exp(1, 1)
            expert_in(2, 2)
            expert_out(0, 0, 0)

            def expert_step(e, u, i):
                expert_exp(e, u)
                expert_in(e + 1, (u + 1) % 3)
                expert_out(e - 1, (u + 2) % 3, i - (1 if u == 0 else 0))

            for e in (2, 3):
                expert_step(e, e % 3, e // 3)
            with act.Fori(1, 4) as i:
                for u in range(1, 4):
                    expert_step(i * 3 + u, u % 3, i + u // 3)
            for e in (13, 14):
                expert_step(e, e % 3, e // 3)
            expert_exp(15, 0)
            expert_out(14, 2, 4)
            expert_out(15, 0, 5)

            act.wait_ge(flag_ready, 1)
            over = act.value_load(flag[0:1, 0:1], min_val=0, max_val=1)
            with act.If(over > 0):
                act.wait_ge(y_out[0], 96)
                with act.Fori(0, NE * (NCH - 1)) as n:
                    act.wait_ge(ov_gu, n + 1)
                    A(sgm[:, 0, :], GU[0][:, 0:2 * C], ACT.Exp, scale=-1.0).then_inc(ov_sg, 1)

        @block.vector
        def _(dve):
            V = nc.vector
            nf = [0]
            steps = [0]

            def full():
                k = nf[0]
                nf[0] += 1
                dve.wait_ge(dve_full, k + 1)
                return RING_D[k % 3]

            def link(ins):
                steps[0] += 1
                ins.then_inc(dve_step, 1)
                dve.wait_ge(dve_step, steps[0])

            pows = [0]

            def norm(t, signal):
                V.bn_stats(st[0:TR, 0:6], xn[0:TR, t, 0:512])
                link(V.bn_stats(st[0:TR, 6:12], xn[0:TR, t, 512:D]))
                pows[0] += 1
                V.bn_aggr(agg[0:TR, :], st[0:TR, :]).then_inc(var_ready, 1)
                dve.wait_ge(var_ready, pows[0])
                link(V.scalar_tensor_tensor(xn[0:TR, t, :], xn[0:TR, t, :], agg[0:TR, 0:1], gb[0:TR, 0, :], ALU.subtract, ALU.mult))
                dve.wait_ge(rstd_ready, pows[0])
                V.scalar_tensor_tensor(xn[0:TR, t, :], xn[0:TR, t, :], rstd[0:TR, 0:1], gb[0:TR, 1, :], ALU.mult, ALU.add).then_inc(signal, 1)

            dve.wait_ge(x_in, 96)
            dve.wait_ge(emb_in, 32)
            for t in range(NT):
                norm(t, x0_ready)
            bk = full()
            cT = bk[:, 0:4 * NS * NPOOL].rearrange("p (g b r) -> p g b r", g=4, b=NS)
            for g in range(4):
                w = 2 << g
                last = V.tensor_reduce(csum[:, g, :], cT[:, g, :, NPOOL - (w - 1):NPOOL], AX, ALU.add)
            last.then_inc(dve_free, 1)
            dve.wait_ge(con_in, 16)
            V.tensor_copy(trib[:, :], con[0:TR, 128:128 + TR])

            dve.wait_ge(rows_act, 1)
            V.memset(zrow, 0.0)
            link(V.tensor_scalar(brow, frow, 0.0, None, ALU.min))
            link(V.tensor_tensor(frow, brow, trow, ALU.subtract))
            link(V.tensor_tensor_scan(brow[:, 0:NP_], frow[:, 0:NP_], zrow[:, 0:NP_], 0.0, ALU.add, ALU.add))
            link(V.tensor_tensor(irow[:, 0:NP_], irow[:, 0:NP_], brow[:, 0:NP_], ALU.subtract))
            link(V.tensor_tensor_scan(mrow[:, 0:NP_], irow[:, 0:NP_], irow[:, 0:NP_], 0.0, ALU.max, ALU.max))
            link(V.tensor_tensor(trow[:, 0:NP_], brow[:, 0:NP_], mrow[:, 0:NP_], ALU.add))
            V.tensor_copy(colv[0:4, 11:12], trow[:, NP_ - 1:NP_]).then_inc(rows_dve, 1)
            V.tensor_scalar(mrow[:, 0:NP_], mrow[:, 0:NP_], -1.0, None, ALU.mult).then_inc(rows_dve, 1)

            for t in range(NT):
                bk = full()
                src = bk[0:TR, :].rearrange("p (h c) -> p h c", h=H)
                if t == NT - 1:
                    V.tensor_copy(vsn, bk[LAST:TR, :])
                V.tensor_copy(vn[0:TR, t, :, 0:HD], src).then_inc(dve_free, 1)
            bk = full()
            dve.wait_ge(memset_done, 1)
            for t in range(NT):
                r = rows_of(t)
                V.tensor_copy(gcol[0:r, 4 * t:4 * t + 4], bk[0:r, 4 * t:4 * t + 4])
                V.tensor_copy(gcol[0:r, 20 + 4 * t:24 + 4 * t], bk[0:r, 20 + 4 * t:24 + 4 * t])
            V.tensor_copy(sg8[:, 0:8], bk[0:NS, 40:48]).then_inc(dve_free, 1)
            bk = full()
            V.tensor_copy(qsn, bk[0:NS, :]).then_inc(dve_free, 1)
            bk = full()
            V.tensor_copy(ksn, bk[0:NS, :]).then_inc(dve_free, 1)
            bk = full()
            V.tensor_copy(vsT[:, :, :], bk[:, 0:H * NS].rearrange("p (h b) -> p h b", h=H)).then_inc(dve_free, 1)
            dve.wait_ge(dve_free, nf[0])
            dve.wait_ge(st_in, 32)
            link(V.tensor_tensor(sg8[:, 24:28], sg8[:, 4:8], sg8[:, 28:32], ALU.add))
            link(V.tensor_tensor(sg8[:, 8:12], sg8[:, 24:28], sg8[:, 0:4], ALU.max))
            link(V.tensor_tensor(sg8[:, 12:16], sg8[:, 0:4], sg8[:, 8:12], ALU.subtract))
            V.tensor_tensor(sg8[:, 16:20], sg8[:, 24:28], sg8[:, 8:12], ALU.subtract).then_inc(sgate_dif, 1)
            offs = [0]
            for t in range(NT):
                offs.append(offs[-1] + NP_ - t * TR)

            def products(h):
                for t in range(NT):
                    r = rows_of(t)
                    bk = full()
                    dve.wait_ge(wexp_done, NT * h + t + 1)
                    blk = pst[0:r, offs[t]:offs[t + 1]]
                    V.tensor_tensor(blk, bk[0:r, 0:NP_ - t * TR], blk, ALU.mult).then_inc(dve_free, 1)
                for q in range(2):
                    bk = full()
                    for t in (range(4) if q == 0 else (4,)):
                        r = rows_of(t)
                        last = V.tensor_scalar(kw[0:r, t, :], bk[0:r, (t % 4) * 128:(t % 4) * 128 + 128], wcol[0:r, t, h:h + 1], None, ALU.mult)
                    last.then_inc(dve_free, 1)

            products(0)
            dve.wait_ge(sgate_exp, 1)
            dve.wait_ge(dve_free, nf[0])
            v4 = lambda x: x.rearrange("p (h c) -> p h c", h=H)
            b4 = lambda x: x.unsqueeze(2).broadcast_to([NS, H, HD])
            pr = P[0:NS, 14830:14830 + 512]
            link(V.tensor_tensor(pr, qsn, ksn, ALU.mult))
            link(V.tensor_reduce(sg8[:, 32:36], v4(pr), AX, ALU.add))
            link(V.tensor_tensor(pr, qsn, n0, ALU.mult))
            link(V.tensor_reduce(sg8[:, 36:40], v4(pr), AX, ALU.add))
            link(V.tensor_tensor(sg8[:, 32:36], sg8[:, 32:36], sg8[:, 12:16], ALU.mult))
            link(V.tensor_tensor(sg8[:, 36:40], sg8[:, 36:40], sg8[:, 16:20], ALU.mult))
            link(V.tensor_tensor(sg8[:, 36:40], sg8[:, 36:40], sg8[:, 32:36], ALU.add))
            link(V.scalar_tensor_tensor(sg8[:, 40:44], sg8[:, 36:40], -1.0, sg8[:, 36:40], ALU.mult, ALU.max))
            link(V.tensor_tensor(sg8[:, 40:44], sg8[:, 40:44], sg8[:, 20:24], ALU.max))
            link(V.reciprocal(sg8[:, 40:44], sg8[:, 40:44]))
            link(V.tensor_tensor(v4(ksn), v4(ksn), b4(sg8[:, 12:16]), ALU.mult))
            link(V.tensor_tensor(v4(n0), v4(n0), b4(sg8[:, 16:20]), ALU.mult))
            V.tensor_tensor(n0, n0, ksn, ALU.add).then_inc(snat_ready, 1)
            link(V.tensor_tensor(v4(vsn), v4(vsn), b4(sg8[:, 32:36]), ALU.mult))

            def take_state(h):
                bk = full()
                if h >= 1:
                    dve.wait_ge(c_out, 32 * h)
                V.tensor_copy(Cout[:, 0:HD], bk[:, 0:HD])
                V.tensor_copy(Cout[0:1, HD:2 * HD], bk[0:1, HD:2 * HD]).then_inc(dve_free, 1)

            def head_norm1(h):
                dve.wait_ge(act_free, at["numerators", h])
                x = hn[0:TR, h % 2]
                qn = x[:, :, HD:HD + 1].rearrange("p t c -> p (t c)")
                d0 = den[0:TR, 0, :]
                link(V.scalar_tensor_tensor(d0, qn, -1.0, qn, ALU.mult, ALU.max))
                fl = gcol[0:TR, 20 + h:40:4]
                link(V.tensor_tensor(d0, d0, fl, ALU.max))
                link(V.reciprocal(d0, d0))
                link(V.tensor_tensor(x[:, :, 0:HD], x[:, :, 0:HD], d0.unsqueeze(2).broadcast_to([TR, NT, HD]), ALU.mult))
                for t in range(NT):
                    last = V.bn_stats(hst[0:TR, t, :], x[:, t, 0:HD])
                link(last)
                for t in range(NT):
                    last = V.bn_aggr(hagg[0:TR, t, :], hst[0:TR, t, :])
                last.then_inc(hs_var, 1)

            def head_norm2(h):
                dve.wait_ge(hs_rstd, h + 1)
                dve.wait_ge(hs_var, h + 1)
                for t in range(NT):
                    r = rows_of(t)
                    last = V.tensor_scalar(hn[0:r, h % 2, t, 0:HD], hn[0:r, h % 2, t, 0:HD], hagg[0:r, t, 0:1], den[0:r, 1, t:t + 1], ALU.subtract, ALU.mult)
                last.then_inc(hn_ready, 1)

            def take_heads(h):
                bk = full()
                dve.wait_ge(sig_done, h // 2 + 1)
                V.scalar_tensor_tensor(mixT[:, 4 + h, 0:NP_], bk[:, :], colv[:, 4 + h:5 + h], sgT[:, h, 0:NP_], ALU.mult, ALU.mult).then_inc(dve_free, 1)

            def carried(b):
                dve.wait_ge(c_in[b % 2], 32 * (b // 2 + 1))
                for h in range(H):
                    last = V.tensor_tensor_reduce(out=Cq_b[b % 2][:, h, :], in0=Cs[b % 2][:, h, :], in1=Cq_b[b % 2][:, h, :], scale=1.0, scalar=0.0,
                                                  op0=ALU.mult, op1=ALU.add, accum_out=cq[:, h, b:b + 1])
                last.then_inc(cq_done, 1)

            def take_last(i):
                bk = full()
                V.tensor_copy(un[0:NPOOL + NS, 256 * i:256 * i + 256], bk[0:NPOOL + NS, 0:256]).then_inc(dve_free, 1)

            def pool_diff(g):
                w = 2 << g
                dve.wait_ge(usum_done, g + 1)
                s = pp[:, g % 2, PADC:PADC + NP_]
                u = uT[:, g, PADC:PADC + NP_]
                us = uT[:, g, PADC + NP_:PADC + NTOK]
                link(V.tensor_tensor(s[:, 0:16], s[:, 0:16], invc[:, g, :], ALU.mult))
                V.scalar_tensor_tensor(u[:, 16:], s[:, 16:], 1.0 / w, u[:, 16:], ALU.mult, ALU.subtract)
                V.tensor_tensor(u[:, 0:16], s[:, 0:16], u[:, 0:16], ALU.subtract)
                link(V.tensor_tensor(csum[:, g, :], csum[:, g, :], us, ALU.add))
                V.scalar_tensor_tensor(us, csum[:, g, :], 1.0 / w, us, ALU.mult, ALU.subtract).then_inc(dif_done, 1)

            carried(0)
            take_state(0)
            head_norm1(0)
            products(1)
            carried(1)
            carried(2)
            head_norm2(0)
            take_heads(0)
            take_state(1)
            head_norm1(1)
            products(2)
            carried(3)
            carried(4)
            head_norm2(1)
            take_heads(1)
            take_last(0)
            take_state(2)
            head_norm1(2)
            products(3)
            head_norm2(2)
            carried(5)
            pool_diff(0)
            carried(6)
            pool_diff(1)
            take_heads(2)
            take_last(1)
            carried(7)
            pool_diff(2)
            take_state(3)
            head_norm1(3)
            pool_diff(3)
            head_norm2(3)
            take_heads(3)

            def residual(t, signal):
                for q in range(2):
                    bk = full()
                    x = xn[0:TR, t, q * 512:q * 512 + 512]
                    V.scalar_tensor_tensor(x, x, ALPHA, bk[0:TR, :], ALU.mult, ALU.add).then_inc(dve_free, 1)
                dve.wait_ge(dve_free, nf[0])
                norm(t, signal)

            dve.wait_ge(gb_in, 32)
            residual(0, x1_ready)
            residual(1, x1_ready)
            bk = full()
            ck = P[0:NS, 10964:10964 + 512]
            link(V.tensor_tensor(v4(ck), v4(bk[0:NS, :]), b4(sg8[:, 16:20]), ALU.mult))
            V.tensor_tensor(vsn, vsn, ck, ALU.add).then_inc(dve_free, 1)
            dve.wait_ge(dve_free, nf[0])
            link(V.tensor_tensor(v4(vsn), v4(vsn), b4(sg8[:, 40:44]), ALU.mult))
            for h in range(H):
                last = V.bn_stats(hst[0:NS, h, :], vsn[:, h * HD:h * HD + HD])
            link(last)
            for h in range(H):
                last = V.bn_aggr(hagg[0:NS, h, :], hst[0:NS, h, :])
            last.then_inc(hs_var, 1)
            dve.wait_ge(hs_rstd, H + 1)
            dve.wait_ge(hs_var, H + 1)
            for h in range(H):
                x = vsn[:, h * HD:h * HD + HD]
                last = V.tensor_scalar(x, x, hagg[0:NS, h, 0:1], den[0:NS, 1, h:h + 1], ALU.subtract, ALU.mult)
            last.then_inc(hs_ready, 1)
            residual(2, x1_ready)
            bk = full()
            for h in range(H):
                last = V.scalar_tensor_tensor(mixT[:, 4 + h, NP_:NTOK], bk[:, h * NS:h * NS + NS], colv[:, 4 + h:5 + h], sgT[:, h, NP_:NTOK], ALU.mult, ALU.mult)
            last.then_inc(dve_free, 1)
            residual(3, x1_ready)
            residual(4, x1_ready)

            NQ = NT * 4

            def finish_probs(n):
                dve.wait_ge(act_free, at["attend", n])
                s = n % 4
                link(V.reciprocal(mx4[0:TR, 8 + s:9 + s], mx4[0:TR, 4 + s:5 + s]))
                V.tensor_scalar(Er[0:TR, s, :], Er[0:TR, s, :], mx4[0:TR, 8 + s:9 + s], None, ALU.mult).then_inc(prob_ready, 1)

            def sample_scores(b):
                dve.wait_ge(kq_done, 2 * b + 2)
                V.tensor_reduce(sS[:, :, 4 * b:4 * b + 4], kvr[:, b % 3].rearrange("p m (h e) -> p m h e", h=4), AX, ALU.add).then_inc(k_used, 1)

            for n in range(NQ):
                k = at["attend", n] - 1
                dve.wait_ge(act_full, k + 1)
                V.tensor_reduce(mx4[0:TR, n % 4:n % 4 + 1], RING_A[k % 3][0:TR, 0:NM], AX, ALU.max, negate=True).then_inc(nmax_done, 1)
                if n >= 1:
                    finish_probs(n - 1)
                if n % 2 == 1 and n // 2 < NS:
                    sample_scores(n // 2)
            finish_probs(NQ - 1)
            bk = full()
            assert nf[0] == at["sample scores"]
            V.tensor_reduce(mx4[0:32, 0:1], bk[0:32, 0:NM], AX, ALU.max, negate=True).then_inc(s_nmax, 1)
            dve.wait_ge(s_exp, 1)
            V.reciprocal(mx4[0:32, 8:9], mx4[0:32, 4:5]).then_inc(dve_free, 1)
            dve.wait_ge(dve_free, nf[0])
            V.tensor_scalar(Es, Es, mx4[0:32, 8:9], None, ALU.mult).then_inc(s_prob, 1)
            bk = full()
            dve.wait_ge(paz_zero, 1)
            for m in range(2):
                diag = paz[:, m].rearrange("p r c -> p (r c)")[:, 0:32 * 32:33]
                last = V.tensor_copy(diag, bk[:, m * 32:m * 32 + 32])
            last.then_inc(dve_free, 1)
            bk = full()
            dve.wait_ge(sn_out, 16)
            V.tensor_copy(ctxs, bk[0:32, 0:CE]).then_inc(dve_free, 1)
            bk = full()
            for ec in range(2):
                src = bk[:, ec * 32:ec * 32 + 32].rearrange("p (b h) -> p h b", h=4)
                last = V.tensor_copy(ctxT.rearrange("p (h e) c -> p h e c", e=2)[:, :, ec, NP_:NTOK], src)
            last.then_inc(dve_free, 1)

            def take_logits(t):
                bk = full()
                V.tensor_copy(rt[:, t, 0:20], bk[0:TR, 0:20]).then_inc(dve_free, 1)

            dve.wait_ge(gb_in, 64)
            for t in range(NT):
                residual(t, x2_ready)
                if t >= 2:
                    take_logits(t - 2)
            take_logits(NT - 2)
            take_logits(NT - 1)

            dve.wait_ge(dve_free, nf[0])
            g = rt[:, :, 0:4]
            e16 = rt[:, :, 4:20]
            gx, og, o1, o2 = rt[:, :, 20:24], rt[:, :, 24:28], rt[:, :, 28:32], rt[:, :, 32:36]
            ein, O1, O2 = rt[:, :, 36:40], rt[:, :, 40:56], rt[:, :, 56:72]
            tmp = rt[:, :, 72:88]
            one = lambda i: rt[:, :, 88 + i:89 + i]
            gmax, m1, m2, acc, pg, xx, g1, g2 = [one(i) for i in range(8)]
            sc4 = lambda x: x.broadcast_to([TR, NT, 4])

            def first_of(x):
                link(V.tensor_copy(acc, x[:, :, 0:1]))
                for j in range(1, 4):
                    xj = x[:, :, j:j + 1]
                    link(V.tensor_tensor(xj, xj, acc, ALU.is_gt))
                    if j < 3:
                        link(V.tensor_tensor(acc, acc, xj, ALU.add))

            link(V.tensor_reduce(gmax, g, AX, ALU.max))
            V.tensor_tensor(gx, g, sc4(gmax), ALU.subtract).then_inc(rt_dve, 1)
            link(V.tensor_tensor(og, g, sc4(gmax), ALU.is_equal))
            first_of(og)
            gj = lambda x: x.rearrange("p t (g j) -> p t g j", g=NG)
            for j in range(EG):
                link(V.tensor_tensor(gj(tmp)[:, :, :, j], gj(e16)[:, :, :, j], og, ALU.mult))
            link(V.tensor_reduce(ein, tmp.rearrange("p t (g j) -> p t j g", g=NG), AX, ALU.add))
            link(V.tensor_reduce(m1, ein, AX, ALU.max))
            link(V.tensor_tensor(o1, ein, sc4(m1), ALU.is_equal))
            first_of(o1)
            link(V.scalar_tensor_tensor(ein, o1, BIG, ein, ALU.mult, ALU.add))
            link(V.tensor_reduce(m2, ein, AX, ALU.max))
            V.tensor_tensor(xx, m2, m1, ALU.subtract).then_inc(rt_dve, 1)
            link(V.tensor_tensor(o2, ein, sc4(m2), ALU.is_equal))
            first_of(o2)
            for j in range(EG):
                link(V.tensor_tensor(gj(O1)[:, :, :, j], og, sc4(o1[:, :, j:j + 1]), ALU.mult))
                link(V.tensor_tensor(gj(O2)[:, :, :, j], og, sc4(o2[:, :, j:j + 1]), ALU.mult))
            V.tensor_tensor(Mb16[:, :, :], O1, O2, ALU.add).then_inc(mask_ready, 1)
            dve.wait_ge(rt_act, 2)
            link(V.tensor_reduce(pg, gx, AX, ALU.add))
            link(V.reciprocal(pg, pg))
            link(V.tensor_scalar(g1, xx, 1.0, None, ALU.add))
            link(V.reciprocal(g1, g1))
            link(V.tensor_tensor(g1, g1, pg, ALU.mult))
            link(V.tensor_tensor(g2, g1, xx, ALU.mult))
            bk = full()
            base = con[0:TR, 296:312].unsqueeze(1).broadcast_to([TR, NT, NE])
            link(V.scalar_tensor_tensor(tmp, bk[0:TR, 0:NT * NE].rearrange("p (t e) -> p t e", t=NT), float(NE), base, ALU.mult, ALU.add))
            V.tensor_reduce(acc[0:1, 0, :], bk[0:1, NT * NE:(NT + 1) * NE], AX, ALU.max).then_inc(dve_free, 1)
            dve.wait_ge(dve_free, nf[0])
            link(V.tensor_scalar(acc[0:1, 0, :], acc[0:1, 0, :], float(C), None, ALU.is_gt))
            V.tensor_copy(flag[0:1, 0:1], acc[0:1, 0, :]).then_inc(flag_ready, 1)
            link(V.tensor_tensor(O1, O1, tmp, ALU.mult))
            link(V.tensor_tensor(O2, O2, tmp, ALU.mult))
            link(V.tensor_reduce(m1, O1, AX, ALU.add))
            link(V.tensor_reduce(m2, O2, AX, ALU.add))
            link(V.tensor_copy(dst[:, 0, :], m1.rearrange("p t c -> p (t c)")))
            V.tensor_copy(dst[:, 1, :], m2.rearrange("p t c -> p (t c)")).then_inc(dst_ready, 1)

            GU = [ps[2], ps[3], ps[6]]

            def expert_in(e, s):
                dve.wait_ge(xgT_full, e * 2 + 2)
                V.tensor_copy(xgT[:, s, 4:8, :], ps[1][:, :].rearrange("p (k c) -> p k c", k=4)).then_inc(xgT_dve, 1)

            def expert_hidden(e, s):
                dve.wait_ge(sgm_ready, e + 1)
                x = sgm[:, 0, :]
                V.tensor_scalar(x, x, 1.0, None, ALU.add).then_inc(hsteps, 1)
                dve.wait_ge(hsteps, e * 3 + 1)
                V.reciprocal(x, x).then_inc(hsteps, 1)
                dve.wait_ge(hsteps, e * 3 + 2)
                V.tensor_tensor(x, x, GU[s][:, 0:2 * C], ALU.mult).then_inc(hsteps, 1)
                dve.wait_ge(hsteps, e * 3 + 3)
                V.tensor_tensor(hh[:, s].rearrange("p f c -> p (f c)"), x, GU[s][:, 2 * C:4 * C], ALU.mult).then_inc(hh_ready, 1)

            def expert_out(e, s, k):
                dve.wait_ge(y_full, e + 1)
                if not (isinstance(k, int) and k == 0):
                    dve.wait_ge(y_out[s], k * 16)
                V.tensor_copy(ysb[:, s, 512:D], ps[5][:, :]).then_inc(y_dve, 1)

            expert_in(0, 0)
            expert_hidden(0, 0)
            expert_in(1, 1)
            expert_hidden(1, 1)
            expert_in(2, 2)
            expert_out(0, 0, 0)

            def expert_step(e, u, i):
                expert_hidden(e, u)
                expert_in(e + 1, (u + 1) % 3)
                expert_out(e - 1, (u + 2) % 3, i - (1 if u == 0 else 0))

            for e in (2, 3):
                expert_step(e, e % 3, e // 3)
            with dve.Fori(1, 4) as i:
                for u in range(1, 4):
                    expert_step(i * 3 + u, u % 3, i + u // 3)
            for e in (13, 14):
                expert_step(e, e % 3, e // 3)
            expert_hidden(15, 0)
            expert_out(14, 2, 4)
            expert_out(15, 0, 5)

            over = dve.value_load(flag[0:1, 0:1], min_val=0, max_val=1)
            with dve.If(over > 0):
                dve.wait_ge(y_out[0], 96)
                with dve.Fori(0, NE * (NCH - 1)) as n:
                    dve.wait_ge(ov_t, n + 1)
                    V.tensor_copy(xgT[:, 0, 0:4, :], ps[0][:, :].rearrange("p (k c) -> p k c", k=4)).then_inc(ovs, 1)
                    V.tensor_copy(xgT[:, 0, 4:8, :], ps[1][:, :].rearrange("p (k c) -> p k c", k=4)).then_inc(ov_tc, 1)
                    dve.wait_ge(ov_sg, n + 1)
                    x = sgm[:, 0, :]
                    V.tensor_scalar(x, x, 1.0, None, ALU.add).then_inc(ovs, 1)
                    dve.wait_ge(ovs, n * 5 + 2)
                    V.reciprocal(x, x).then_inc(ovs, 1)
                    dve.wait_ge(ovs, n * 5 + 3)
                    V.tensor_tensor(x, x, GU[0][:, 0:2 * C], ALU.mult).then_inc(ovs, 1)
                    dve.wait_ge(ovs, n * 5 + 4)
                    V.tensor_tensor(hh[:, 0].rearrange("p f c -> p (f c)"), x, GU[0][:, 2 * C:4 * C], ALU.mult).then_inc(ov_h, 1)
                    dve.wait_ge(ov_y, n + 1)
                    V.tensor_copy(ysb[:, 0, 0:512], ps[4][:, :]).then_inc(ovs, 1)
                    V.tensor_copy(ysb[:, 0, 512:D], ps[5][:, :]).then_inc(ov_yc, 1)
                    dve.wait_ge(ov_out, n * 16 + 16)

            dve.wait_ge(gb_in, 96)
            for t in range(NT):
                dve.wait_ge(yg_in[t % 2], 32 * (t // 2 + 1))
                dve.wait_ge(xa_ready, t + 1)
                x = xn[0:TR, t, :]
                link(V.scalar_tensor_tensor(x, yg[0:TR, t % 2, 0, :], g1[:, t, :], x, ALU.mult, ALU.add))
                V.scalar_tensor_tensor(x, yg[0:TR, t % 2, 1, :], g2[:, t, :], x, ALU.mult, ALU.add).then_inc(yg_used, 1)
                dve.wait_ge(yg_used, t + 1)
                norm(t, x3_ready)

        @block.gpsimd
        def _(pool):
            G = nc.gpsimd
            steps = [0]

            def link(ins):
                steps[0] += 1
                ins.then_inc(pool_step, 1)
                pool.wait_ge(pool_step, steps[0])

            link(G.memset(half[:, :], -0.5))
            G.memset(turn[:, :], 0.0)
            G.memset(onesb[:, :], 1.0)
            link(G.memset(wg[:, :, :], 0.0))
            win = a["w_in"][0].rearrange("(k p) c -> p k c", p=128)
            GO = PW + 4 * 512
            pool.dma_start(wg[:, :, 0:4], win[:, :, GO:GO + 4]).then_inc(wgr_in, 16)
            pool.dma_start(wg[:, :, 32:36], win[:, :, GO + 4:GO + 8]).then_inc(wgr_in, 16)
            pool.dma_start(wr[:, :, 0:4], a["w_gr"][0].rearrange("(k p) c -> p k c", p=128)).then_inc(wgr_in, 16)
            pool.dma_start(wr[:, :, 4:20], a["w_er"][0].rearrange("(k p) c -> p k c", p=128)).then_inc(wgr_in, 16)
            col = lambda ap: ap.rearrange("(c one) -> c one", one=1)
            pool.dma_start(colv[0:4, 8:9], col(a["b_i"][0])).then_inc(small_in, 16)
            pool.dma_start(colv[32:36, 9:10], col(a["b_f"][0])).then_inc(small_in, 16)
            pool.dma_start(colv[0:4, 10:11], col(a["b_gr"][0])).then_inc(small_in, 16)
            pool.dma_start(colv[4:20, 10:11], col(a["b_er"][0])).then_inc(small_in, 16)
            for g in range(4):
                pool.dma_start(colv[:, g:g + 1], col(a["pool_scale"][0, g * 128:g * 128 + 128])).then_inc(small_in, 16)
                pool.dma_start(colv[:, 4 + g:5 + g], col(a["mlstm_norm_g"][0, g * 128:g * 128 + 128])).then_inc(small_in, 16)
            pool.dma_start(poolw[:, :, :], a["pool_w"][0].rearrange("g c e -> c g e")).then_inc(small_in, 16)
            pool.dma_start(n0, a["state_mlstm_n"][0].rearrange("b h k -> b (h k)")).then_inc(st_in, 16)
            pool.dma_start(sg8[:, 28:32], a["state_mlstm_m"][0]).then_inc(st_in, 16)

            pows = [0]

            def norm_rstd():
                pows[0] += 1
                pool.wait_ge(var_ready, pows[0])
                link(G.tensor_scalar(rstd[0:TR, 0:1], agg[0:TR, 1:2], LN_EPS, None, ALU.add))
                G.tensor_tensor(rstd[0:TR, 0:1], rstd[0:TR, 0:1], half[0:TR, 0:1], ALU.pow).then_inc(rstd_ready, 1)

            for t in range(NT):
                norm_rstd()
            G.memset(uT[:, :, 0:PADC], 0.0)
            G.memset(pp[:, :, 0:PADC], 0.0)
            G.memset(hn[:, :, :, :], 1.0)
            G.memset(gcol[:, :], 1.0)
            G.memset(vn[:, :, :, HD:HD + 1], 1.0)
            G.memset(tokz[:, :], 0.0)
            G.iota(tok[:, :].bitcast(I32), pattern=[[TR, NT]], base=0, channel_multiplier=1).then_inc(memset_done, 1)
            pool.wait_ge(memset_done, 1)
            pool.dma_start(lst_d.rearrange("(p r) one -> p (r one)", p=128), tokz.bitcast(U32)).then_inc(lst_zero, 16)

            def masks(h):
                offs = [0]
                for t in range(NT):
                    offs.append(offs[-1] + NP_ - t * TR)
                for t in range(NT):
                    pool.wait_ge(dve_free, at["scores", h, t])
                    r = rows_of(t)
                    blk = pst[0:r, offs[t]:offs[t] + r]
                    G.affine_select(blk, blk, pattern=[[1, r]], compare_op=ALU.is_ge, fill=0.0, base=0, channel_multiplier=-1).then_inc(sel_done, 1)

            def head_rstd(h, n, m):
                pool.wait_ge(hs_var, h + 1)
                link(G.tensor_scalar(den[0:n, 1, 0:m], hagg[0:n, 0:m, 1:2].rearrange("p t c -> p (t c)"), LN_EPS, None, ALU.add))
                G.tensor_tensor(den[0:n, 1, 0:m], den[0:n, 1, 0:m], half[0:n, 0:m], ALU.pow).then_inc(hs_rstd, 1)

            def state_out(h):
                pool.wait_ge(dve_free, at["state", h])
                pool.dma_start(o_pC[0, 0, h], Cout[:, 0:HD]).then_inc(c_out, 16)
                pool.dma_start(o_pn[0, 0, h:h + 1], Cout[0:1, HD:2 * HD]).then_inc(c_out, 16)

            def load_state(b):
                if b >= 2:
                    pool.wait_ge(c_store[b % 2], 16 * (b // 2))
                pool.dma_start(Cs[b % 2], a["state_mlstm_C"][0, b].rearrange("h v k -> v h k")).then_inc(c_in[b % 2], 16)
                pool.dma_start(qk_b[b % 2], qk_d[b].partition_broadcast(128)).then_inc(c_in[b % 2], 16)

            def update_state(b):
                pool.wait_ge(cq_done, b + 1)
                wv = wcb[:, b, :].unsqueeze(2).broadcast_to([128, H, HD])
                vv = vsT[:, :, b:b + 1].broadcast_to([128, H, HD])
                c, k = Cs[b % 2], Ck_b[b % 2]
                G.tensor_tensor(c, c, wv, ALU.mult)
                link(G.tensor_tensor(k, k, vv, ALU.mult))
                G.tensor_tensor(c, c, k, ALU.add).then_inc(cupd_done, 1)
                pool.wait_ge(cupd_done, b + 1)
                pool.dma_start(o_sC[0, b].rearrange("h v k -> v h k"), c).then_inc(c_store[b % 2], 16)

            def window_sums(g):
                pool.wait_ge(act_free, at["u", g // 2])
                src = uT[:, g]
                if g >= 1:
                    pool.wait_ge(dif_done, g)
                for j in range(g + 1):
                    d = pp[:, j % 2]
                    s = 1 << j
                    ins = G.tensor_tensor(d[:, PADC:PADC + NP_], src[:, PADC:PADC + NP_], src[:, PADC - s:PADC + NP_ - s], ALU.add)
                    if j < g:
                        link(ins)
                    src = d
                ins.then_inc(usum_done, 1)

            pool.wait_ge(rows_dve, 1)
            pool.dma_start(o_pm[0, 0].rearrange("(c one) -> c one", one=1), colv[0:4, 11:12]).then_inc(out_done, 16)
            masks(0)
            pool.wait_ge(snat_ready, 1)
            pool.dma_start(qk_d[:, 0:512], qsn).then_inc(bounce, 16)
            pool.dma_start(qk_d[:, 512:1024], ksn).then_inc(bounce, 16)
            pool.dma_start(swc_d, sg8[:, 16:20]).then_inc(bounce, 16)
            pool.dma_start(o_sn[0].rearrange("b h k -> b (h k)"), n0).then_inc(sn_out, 16)
            pool.dma_start(o_sm[0], sg8[:, 8:12]).then_inc(out_done, 16)
            pool.wait_ge(bounce, 48)
            pool.dma_start(wcb[:, :, :].rearrange("p b h -> p (b h)"), swc_d.rearrange("b h -> (b h)").partition_broadcast(128)).then_inc(bounce, 16)
            pool.wait_ge(bounce, 64)
            pool.wait_ge(lst_zero, 16)
            load_state(0)
            load_state(1)
            update_state(0)
            load_state(2)
            head_rstd(0, TR, NT)
            masks(1)
            for b in (1, 2):
                update_state(b)
            state_out(0)
            for b in (3, 4):
                load_state(b)
            head_rstd(1, TR, NT)
            masks(2)
            for b in (3, 4):
                update_state(b)
            state_out(1)
            for b in (5, 6):
                load_state(b)
            head_rstd(2, TR, NT)
            masks(3)
            window_sums(0)
            for b in (5, 6):
                update_state(b)
            load_state(7)
            window_sums(1)
            state_out(2)
            window_sums(2)
            update_state(7)
            window_sums(3)
            head_rstd(3, TR, NT)
            pool.wait_ge(dve_free, at["last u", 1])
            pool.dma_start(o_ppool[0, 0], un[0:NPOOL, :]).then_inc(un_out, 16)
            pool.dma_start(o_spool[0, :, NPOOL - 1, :], un[NPOOL:NPOOL + NS, :]).then_inc(un_out, 16)
            pool.dma_start(o_spool[0, :, 0:NPOOL - 1, :], a["cache_pool"][0, :, 1:NPOOL, :]).then_inc(un_out, 16)
            state_out(3)

            pool.wait_ge(c_out, 32 * H)

            def norm_vectors(gname, bname):
                pool.dma_start(gb[:, 0, :], a[gname][0].partition_broadcast(128)).then_inc(gb_in, 16)
                pool.dma_start(gb[:, 1, :], a[bname][0].partition_broadcast(128)).then_inc(gb_in, 16)

            norm_vectors("ln1_g", "ln1_b")
            norm_rstd()
            norm_rstd()
            head_rstd(4, NS, H)
            for t in range(3):
                norm_rstd()
            pool.wait_ge(x1_ready, NT)
            norm_vectors("ln2_g", "ln2_b")
            pool.wait_ge(act_free, at["sample q"])
            pool.dma_start(sq2_d, qs2).then_inc(sq2_out, 16)
            for b in range(NS):
                pool.wait_ge(kv_in[b % 3], 16 * (b // 3 + 1))
                for hf in range(2):
                    pool.wait_ge(qb_in[hf], 16 * (b + 1))
                    x = kvr[:, b % 3, :, hf * 512:hf * 512 + 512]
                    G.tensor_tensor(x, x, qb[:, hf * 512:hf * 512 + 512].unsqueeze(1).broadcast_to([128, 2, 512]), ALU.mult).then_inc(kq_done, 1)
            pool.wait_ge(sq2_out, 16)
            G.memset(paz, 0.0).then_inc(paz_zero, 1)
            for t in range(NT):
                norm_rstd()
                pool.wait_ge(x2_ready, t + 1)
                pool.dma_start(x2_d[t * TR:t * TR + TR, :], xn[0:TR, t, :]).then_inc(x2_out, 16)
            norm_vectors("ln3_g", "ln3_b")

            pool.wait_ge(dst_ready, 1)
            for t in range(NT):
                for k in range(2):
                    pool.indirect_dma_start(out=lst_d, out_offset=bass.IndirectOffsetOnAxis(ap=dst[:, k, t:t + 1], axis=0),
                                            in_=tok[:, t:t + 1], in_offset=None).then_inc(lst_out, 16)
            pool.wait_ge(lst_out, 16 * 2 * NT)
            pool.dma_start(idxl[:, :], lst_d.rearrange("(r e) one -> r (e one)", e=NE)[0:C, :]).then_inc(idx_in, 16)
            pool.wait_ge(idx_in, 16)
            pool.wait_ge(x2_out, 16 * NT)
            for e in range(NE):
                s = e % 3
                if e >= 3:
                    pool.wait_ge(xgT_full, 2 * (e - 2))
                pool.indirect_dma_start(out=xg[:, s, :], out_offset=None, in_=x2_d,
                                        in_offset=bass.IndirectOffsetOnAxis(ap=idxl[:, e:e + 1], axis=0)).then_inc(xg_in[s], 16)

            pool.wait_ge(flag_ready, 1)
            over = pool.value_load(flag[0:1, 0:1], min_val=0, max_val=1)
            with pool.If(over > 0):
                pool.wait_ge(xgT_full, 2 * NE)
                with pool.Fori(0, NE * (NCH - 1)) as n:
                    pool.wait_ge(ov_idx, n * 16 + 16)
                    G.tensor_tensor(turn[:, 0:1], turn[:, 1:2], turn[:, 1:2], ALU.mult).then_inc(ov_turn, 1)
                    pool.indirect_dma_start(out=xg[:, 0, :], out_offset=None, in_=x2_d,
                                            in_offset=bass.IndirectOffsetOnAxis(ap=idx1[:, 0:1], axis=0)).then_inc(ov_x, 16)
                pool.wait_ge(ov_out, 16 * NE * (NCH - 1))

            for s in range(3):
                pool.wait_ge(y_out[s], 16 * (6 if s == 0 else 5))

            def finish(rows):
                def fetch(t):
                    if t >= 2:
                        pool.wait_ge(yg_used, t - 1)
                    for k in range(2):
                        pool.indirect_dma_start(out=yg[0:TR, t % 2, k, :], out_offset=None, in_=y_d[0:rows, :],
                                                in_offset=bass.IndirectOffsetOnAxis(ap=dst[:, k, t:t + 1], axis=0)).then_inc(yg_in[t % 2], 16)

                fetch(0)
                fetch(1)
                for t in range(NT):
                    norm_rstd()
                    if t + 2 < NT:
                        fetch(t + 2)
                    pool.wait_ge(x3_ready, t + 1)
                    pool.dma_start(o_xp[0, t * TR:t * TR + rows_of(t), :], xn[0:rows_of(t), t, :]).then_inc(out_done, 16)
                pool.dma_start(o_xs.rearrange("b one d -> (b one) d"), xn[LAST:TR, NT - 1, :]).then_inc(out_done, 16)

            before = pows[0], steps[0]
            with pool.If(over > 0):
                finish(NE * R)
            pows[0], steps[0] = before
            with pool.If(over < 1):
                finish(NE * C)


_OUTS = [(1, 512, 1024), (8, 1, 1024), (1, 1, 15, 512), (1, 1, 4, 128, 128), (1, 1, 4, 128), (1, 1, 4),
         (1, 1, 256, 4, 256), (1, 1, 256, 4, 256), (1, 8, 15, 512), (1, 8, 4, 128, 128), (1, 8, 4, 128), (1, 8, 4)]


def kernel(**inputs):
    import concourse.bacc as bacc
    from concourse.bass_utils import run_bass_kernel_spmd

    nc = bacc.Bacc("TRN2", target_bir_lowering=False, num_devices=1)
    arrays, aps = {}, {}
    for name, value in [*inputs.items(), ("consts", constants())]:
        value = np.ascontiguousarray(value)
        arrays[f"in_{name}"] = value
        aps[name] = nc.dram_tensor(f"in_{name}", value.shape, mybir.dt.from_np(value.dtype), kind="ExternalInput").ap()
    outs = [nc.dram_tensor(f"out_{i}", shape, F32, kind="ExternalOutput").ap() for i, shape in enumerate(_OUTS)]
    layer_kernel(nc, aps, outs)
    r = run_bass_kernel_spmd(nc, [arrays], core_ids=[0])
    return tuple(r.results[0][f"out_{i}"] for i in range(len(_OUTS)))
```

```python
import numpy as np
import concourse.bass as bass
from concourse import mybir
from contextlib import ExitStack

F32 = mybir.dt.float32
BF16 = mybir.dt.bfloat16
U32 = mybir.dt.uint32
I32 = mybir.dt.int32
ALU = mybir.AluOpType
ACT = mybir.ActivationFunctionType
AX = mybir.AxisListType.X

D = 1024
NP_, NS = 512, 8
NTOK = NP_ + NS
NT = 5
TR = NTOK // NT
LAST = NP_ - (NT - 1) * TR
KC = D // 128
H, HD = 4, 128
PW = 512
NPOOL = 15
NM = 256
CE = 256
NE, NG, EG = 16, 4, 4
DE = 256
C = 128
NCH = -(-NTOK // C)
R = NCH * C
WR = 3
ROUTED = [(0, 3), (3, 4), (4, NT)]
ALPHA = 2.0 ** 0.25
LN_EPS = 1e-5
GRP = [(0, 3 * TR), (3 * TR, 2 * TR)]
COLS = 316
PADC = 16
BIG = -3.0e38


def rows_of(t):
    return LAST if t == NT - 1 else TR


def constants():
    c = np.zeros((128, COLS), np.float32)
    c[:, 0:128] = np.eye(128, dtype=np.float32)
    c[0:TR, 128:128 + TR] = np.triu(np.ones((TR, TR), np.float32), 1)
    for g in range(4):
        w = 2 << g
        c[:, 232 + 16 * g:248 + 16 * g] = 1.0 / np.minimum(np.arange(16) + 1, w)
    c[:, 296:312] = np.arange(16)
    c[:, 312:316] = [4, 3, 2, 1]
    return c


def layer_kernel(nc, a, o):
    (o_xp, o_xs, o_ppool, o_pC, o_pn, o_pm, o_pmk, o_pmv, o_spool, o_sC, o_sn, o_sm) = o
    ctx = ExitStack()
    with ctx:
        def sb(name, shape, dt=F32):
            return ctx.enter_context(nc.sbuf_tensor(name, shape, dt))

        def sem(name):
            return ctx.enter_context(nc.semaphore(name))

        def dram(name, shape, dt=F32):
            return nc.dram_tensor(name, shape, dt, kind="Internal").ap()

        qk_d = dram("qk_d", [NS, 1024])
        swc_d = dram("swc_d", [NS, H])
        sq2_d = dram("sq2_d", [NS, D])
        x2_d = dram("x2_d", [NTOK, D])
        lst_d = dram("lst_d", [NE * R, 2], U32)
        y_d = dram("y_d", [NE * R, D])
        lst_e = lst_d.rearrange("(r e) w -> r e w", e=NE)
        y_e = y_d.rearrange("(r e) d -> r e d", e=NE)

        xn = sb("xn", [128, NT, D])
        xT = sb("xT", [128, KC, NTOK])
        wring = sb("wring", [128, WR, KC, 512])
        con = sb("con", [128, COLS])
        gb = sb("gb", [128, 2, D])
        mkT = sb("mkT", [128, KC, NM])
        mv = sb("mv", [128, 2, D])
        poolw = sb("poolw", [128, 4, 128])
        wg = sb("wg", [128, KC, 36])
        wr = sb("wr", [128, KC, 20])
        smp = sb("smp", [128, 2560])
        colv = sb("colv", [128, 16])
        gcol = sb("gcol", [128, 48])
        wcol = sb("wcol", [128, NT, H])
        st = sb("st", [128, 12])
        agg = sb("agg", [128, 2])
        rstd = sb("rstd", [128, NT])
        half = sb("half", [128, NT])
        hst = sb("hst", [128, NT, 6])
        hagg = sb("hagg", [128, NT, 2])
        den = sb("den", [128, 2, NT])
        P = sb("P", [128, 21038])
        sg8 = sb("sg8", [NS, 64])
        onesb = sb("onesb", [TR, TR], BF16)
        trib = sb("trib", [TR, TR], BF16)
        ps = [ctx.enter_context(nc.psum_tensor(f"ps{i}", [128, 512], F32)) for i in range(8)]
        RING_A, RING_D, MBANK = ps[0:3], ps[3:6], ps[6:8]

        ident = con[:, 0:128]
        invc = con[:, 232:296].rearrange("p (g c) -> p g c", g=4)

        def view(lo, n, pat=None, **kw):
            v = P[:, lo:lo + n]
            return v.rearrange(pat, **kw) if pat else v

        uw = PADC + NTOK
        uT = view(0, 4 * uw, "p (g c) -> p g c", g=4)
        qT = view(2144, 2080, "p (h c) -> p h c", h=4)
        kT = view(4224, 2080, "p (h c) -> p h c", h=4)
        sgT = view(6304, 2080, "p (h c) -> p h c", h=4)
        vn = view(8384, 2580, "p (t h c) -> p t h c", t=NT, h=H)
        pst = view(10964, 1520)
        pp = view(12484, 1056, "p (b c) -> p b c", b=2)
        hn = view(13540, 1290, "p (b t c) -> p b t c", b=2, t=NT)
        BUF = (1, 0, 1, 0, 0, 1, 1, 1)
        earlier = lambda b: BUF[:b].count(BUF[b])
        Cs = [view(lo, 512, "p (h k) -> p h k", h=H) for lo in (16878, 14830)]
        qk_b = [view(lo + 512, 1024) for lo in (16878, 14830)]
        Cq_b = [x[:, 0:512].rearrange("p (h k) -> p h k", h=H) for x in qk_b]
        Ck_b = [x[:, 512:1024].rearrange("p (h k) -> p h k", h=H) for x in qk_b]
        tokz = view(15854, 2 * NE * R // 128)
        mixT = view(16878, 4160, "p (k c) -> p k c", k=KC)
        memn = view(16878, 2048, "p (m d) -> p m d", m=2)
        mkn = view(16878 + 2048, 2048, "p (m d) -> p m d", m=2)
        memT = view(2144, 2048, "p (k m) -> p k m", k=KC)
        irow, frow, brow, mrow, trow, zrow = [P[0:4, 16878 + 520 * i:16878 + 520 * (i + 1)] for i in range(6)]
        kw = gb[:, 0, 0:640].rearrange("p (t k) -> p t k", t=NT)
        Cout = gb[:, 1, 0:512].rearrange("p (b k) -> p b k", b=2)
        kvr = view(0, 6144, "p (s m d) -> p s m d", s=3, m=2)
        qcT = view(6304, 4160, "p (k c) -> p k c", k=KC)
        paT = view(10464, 4160, "p (h m c) -> p h m c", h=4, m=2)
        Er = view(14830, 1024, "p (s m) -> p s m", s=4)
        qb = view(15854, 1024)
        ctxT = mixT
        dnr = view(0, 6144, "p (s f d) -> p s f d", s=3, f=2)
        xg = view(6304, 3072, "p (s d) -> p s d", s=3)
        xgT = view(9376, 3072, "p (s k c) -> p s k c", s=3, k=KC)
        hh = view(12448, 768, "p (s f c) -> p s f c", s=3, f=2)
        sgm = view(13216, 512, "p (s f) -> p s f", s=2)
        ysb = view(13728, 3072, "p (s d) -> p s d", s=3)
        cache = smp[0:NS * NPOOL, 0:512]
        un = smp[:, 0:512]
        qsn, ksn, vsn, n0 = [smp[0:NS, 512 * i:512 * (i + 1)] for i in range(1, 5)]
        qs2 = smp[0:NS, 0:D]
        paz = smp[:, 0:2048].rearrange("p (m r c) -> p m r c", m=2, r=32)
        ctxs = smp[0:32, 2048:2304]
        Es = poolw[0:32, 0:2, :].rearrange("p a b -> p (a b)")
        sS = poolw[:, 2, 0:64].rearrange("p (m r) -> p m r", m=2)
        csum = sb("csum", [128, 4, NS])
        cq = sb("cq", [128, H, NS])
        vsT = sb("vsT", [128, H, NS])
        wcb = sb("wcb", [128, NS, H])
        mx4 = sb("mx4", [128, 12])
        rt = smp[0:TR, 0:NT * 100].rearrange("p (t c) -> p t c", t=NT)
        lgT = smp[0:20, 512:512 + 2 * TR].rearrange("p (b c) -> p b c", b=2)
        Mb16 = sb("Mb16", [TR, NT, NE], BF16)
        dst = sb("dst", [TR, 2, NT], U32)
        tokg = smp[0:TR, 1024:1024 + 4 * NT].rearrange("p (t k w) -> p t k w", t=NT, k=2)
        lists = smp[0:C, 1056:1056 + 2 * NE].rearrange("p (e w) -> p e w", w=2)
        list1 = smp[0:C, 1090:1092]
        gate3 = smp[0:C, 1096:1099]
        flag = sb("flag", [1, 1], I32)
        most = smp[0:1, 1000:1001]
        turn = smp[0:1, 1001:1003]

        act_full, act_free, dve_full, dve_free = sem("act_full"), sem("act_free"), sem("dve_full"), sem("dve_free")
        dve_step, act_step, pool_step = sem("dve_step"), sem("act_step"), sem("pool_step")
        mem_in = [sem(f"mem_in{m}") for m in range(2)]
        half_in, con_in, x_in, gb_in, small_in, cache_in = [sem(s) for s in ("half_in", "con_in", "x_in", "gb_in", "small_in", "cache_in")]
        wgr_in, st_in, emb_in = sem("wgr_in"), sem("st_in"), sem("emb_in")
        blk_in = [sem(f"blk_in{i}") for i in range(WR)]
        x0_ready, x1_ready, x2_ready, x3_ready = sem("x0_ready"), sem("x1_ready"), sem("x2_ready"), sem("x3_ready")
        x3_centred, x3_scaled, x4_ready, x_out = sem("x3_centred"), sem("x3_scaled"), sem("x4_ready"), sem("x_out")
        var_ready, rstd_ready = sem("var_ready"), sem("rstd_ready")
        out_done = sem("out_done")
        mk_out, mv_out = sem("mk_out"), sem("mv_out")
        memset_done = sem("memset_done")
        rows_act, rows_dve = sem("rows_act"), sem("rows_dve")
        mb_full, wexp_done, sel_done = sem("mb_full"), sem("wexp_done"), sem("sel_done")
        c_out, un_out, sn_out = [sem(f"c_out{i}") for i in range(2)], sem("un_out"), sem("sn_out")
        sig_done = sem("sig_done")
        hn_ready, snat_ready = sem("hn_ready"), sem("snat_ready")
        sgate_dif, sgate_exp = sem("sgate_dif"), sem("sgate_exp")
        usum_done, dif_done = sem("usum_done"), sem("dif_done")
        bounce, cq_done, cupd_done = sem("bounce"), sem("cq_done"), sem("cupd_done")
        c_in = [sem(f"c_in{i}") for i in range(2)]
        c_store = [sem(f"c_store{i}") for i in range(2)]
        hs_var, hs_rstd, hs_ready = sem("hs_var"), sem("hs_rstd"), sem("hs_ready")
        sq2_out, kq_done = sem("sq2_out"), sem("kq_done")
        qb_in = [sem(f"qb_in{i}") for i in range(2)]
        kv_in = [sem(f"kv_in{i}") for i in range(3)]
        k_used, v_used = sem("k_used"), sem("v_used")
        nmax_done, prob_ready = sem("nmax_done"), sem("prob_ready")
        s_nmax, s_exp, s_prob, paz_zero = sem("s_nmax"), sem("s_exp"), sem("s_prob"), sem("paz_zero")
        x2_out = sem("x2_out")
        rt_act, rt_dve = sem("rt_act"), sem("rt_dve")
        mask_ready, dst_ready, lst_zero, lst_out, idx_in = [sem(s) for s in ("mask_ready", "dst_ready", "lst_zero", "lst_out", "idx_in")]
        xg_in = [sem(f"xg_in{i}") for i in range(3)]
        dn_in = [sem(f"dn_in{i}") for i in range(3)]
        xgT_full, xgT_act, xgT_dve = sem("xgT_full"), sem("xgT_act"), sem("xgT_dve")
        gu_full, sgm_ready, hh_ready, y_full = sem("gu_full"), sem("sgm_ready"), sem("hh_ready"), sem("y_full")
        y_act, y_dve = sem("y_act"), sem("y_dve")
        y_out = [sem(f"y_out{i}") for i in range(3)]
        flag_ready, ov_turn = sem("flag_ready"), sem("ov_turn")
        hsteps, ovs = sem("hsteps"), sem("ovs")
        y_added = [sem(f"y_added{t}") for t in range(NT)]
        xa_ready, tok_ready, gate_set = sem("xa_ready"), sem("tok_ready"), sem("gate_set")
        ov_w, ov_idx, ov_x, ov_t, ov_tc, ov_gu, ov_sg, ov_h, ov_y, ov_yc, ov_out = [sem(s) for s in (
            "ov_w", "ov_idx", "ov_x", "ov_t", "ov_tc", "ov_gu", "ov_sg", "ov_h", "ov_y", "ov_yc", "ov_out")]

        block = ctx.enter_context(nc.Block())

        at, used = {}, {}

        def wcols(w, c0, n=512):
            return w[0].rearrange("(k p) c -> p k c", p=128)[:, :, c0:c0 + n]

        BLOCKS = [("wk0", wcols(a["ca_wk"], 0)), ("wk1", wcols(a["ca_wk"], 512)),
                  ("wv0", wcols(a["ca_wv"], 0)), ("wv1", wcols(a["ca_wv"], 512)),
                  ("q", wcols(a["w_in"], PW)), ("k", wcols(a["w_in"], PW + 512)),
                  ("v", wcols(a["w_in"], PW + 1024)), ("og", wcols(a["w_in"], PW + 1536)),
                  ("u", wcols(a["w_in"], 0)),
                  ("wo0", wcols(a["w_out"], 0)), ("wo1", wcols(a["w_out"], 512)),
                  ("wq0", wcols(a["ca_wq"], 0)), ("wq1", wcols(a["ca_wq"], 512)),
                  ("wc0", wcols(a["ca_wo"], 0)), ("wc1", wcols(a["ca_wo"], 512))]
        BI = {name: i for i, (name, _) in enumerate(BLOCKS)}
        NB = len(BLOCKS)
        assert NB % WR == 0
        gate_w = a["w_gate"][0].rearrange("e (k p) f -> p e k f", p=128)
        up_w = a["w_up"][0].rearrange("e (k p) f -> p e k f", p=128)
        down_w = a["w_down"][0].rearrange("e (f p) d -> p e f d", p=128)
        one_expert = lambda w, e: w[:, bass.ds(e, 1)].rearrange("p one k f -> p (one k) f")
        kv_src = [a["cache_mem_k"][0, b] for b in range(NS)] + [a["cache_mem_v"][0, b] for b in range(NS)]

        def add_windows(add, g, link):
            src = uT[:, g]
            for j in range(g + 1):
                d, s = pp[:, j % 2], 1 << j
                ins = add(d[:, PADC:PADC + NP_], src[:, PADC:PADC + NP_], src[:, PADC - s:PADC + NP_ - s], ALU.add)
                if j < g:
                    link(ins)
                src = d
            return ins

        @block.tensor
        def _(pe):
            na, nd = [0], [0]

            def bank_a():
                k = na[0]
                na[0] += 1
                if k >= 3:
                    pe.wait_ge(act_free, k - 2)
                return RING_A[k % 3]

            def bank_d():
                k = nd[0]
                nd[0] += 1
                if k >= 3:
                    pe.wait_ge(dve_free, k - 2)
                return RING_D[k % 3]

            mm = nc.tensor.matmul

            def use_block(name):
                i = BI[name]
                pe.wait_ge(blk_in[i % WR], 16 * (i // WR + 1))
                return wring[:, i % WR]

            def contract(out, lhs, rhs, n=KC):
                for k in range(n):
                    last = mm(out, lhs(k), rhs(k), start=(k == 0), stop=(k == n - 1))
                return last

            def project(name, cts, src=xT, groups=GRP):
                w = use_block(name)
                for ct in cts:
                    for c0, cn in groups:
                        bk = bank_a()
                        last = contract(bk[:, 0:cn], lambda k: w[:, k, ct * 128:ct * 128 + 128],
                                        lambda k: src[:, k, c0:c0 + cn])
                        last.then_inc(act_full, 1)
                used[BI[name]] = (act_full, na[0])

            pe.wait_ge(con_in, 16)
            for m in range(2):
                pe.wait_ge(mem_in[m], 16)
                for q in range(2):
                    bk = bank_a()
                    for k in range(4):
                        last = nc.tensor.transpose(bk[:, k * 128:k * 128 + 128], memn[:, m, (4 * q + k) * 128:(4 * q + k + 1) * 128], ident)
                    last.then_inc(act_full, 1)
            pe.wait_ge(act_free, 4)
            for name in ("wk0", "wk1", "wv0", "wv1"):
                if name == "wk0":
                    pe.wait_ge(half_in, 16)
                    w = wring[:, 0]
                else:
                    w = use_block(name)
                for m in range(2):
                    bk = bank_a()
                    for k in range(KC):
                        if name == "wk0" and k == 4:
                            use_block(name)
                        last = mm(bk[:, :], memT[:, k, m * 128:m * 128 + 128], w[:, k, :], start=(k == 0), stop=(k == KC - 1))
                    last.then_inc(act_full, 1)
                used[BI[name]] = (act_full, na[0])
            pe.wait_ge(cache_in, 16)
            bk = bank_d()
            n = NS * NPOOL
            for g in range(4):
                last = nc.tensor.transpose(bk[:, g * n:g * n + n], cache[:, g * 128:g * 128 + 128], ident[0:n, 0:n])
            last.then_inc(dve_full, 1)
            pe.wait_ge(act_free, 8)
            for m in range(2):
                for q in range(2):
                    bk = bank_a()
                    for k in range(4):
                        last = nc.tensor.transpose(bk[:, k * 128:k * 128 + 128], mkn[:, m, (4 * q + k) * 128:(4 * q + k + 1) * 128], ident)
                    last.then_inc(act_full, 1)

            def transpose_x(t, ready):
                pe.wait_ge(ready, t + 1)
                for q in range(2):
                    bk = bank_a()
                    for k in range(4):
                        last = nc.tensor.transpose(bk[:, k * TR:k * TR + TR], xn[0:TR, t, (4 * q + k) * 128:(4 * q + k + 1) * 128], ident[0:TR, 0:TR])
                    last.then_inc(act_full, 1)

            for t in range(NT):
                transpose_x(t, x0_ready)
            pe.wait_ge(act_free, na[0])
            pe.wait_ge(wgr_in, 64)
            for c0, cn in GRP:
                bk = bank_a()
                contract(bk[0:36, 0:cn], lambda k: wg[:, k, :], lambda k: xT[:, k, c0:c0 + cn]).then_inc(act_full, 1)
            project("q", range(4))
            project("k", range(4))
            qk_groups = na[0]
            w = use_block("v")
            for t in range(NT):
                bk = bank_d()
                contract(bk[0:TR, :], lambda k: xT[:, k, t * TR:t * TR + TR], lambda k: w[:, k, :]).then_inc(dve_full, 1)
            used[BI["v"]] = (dve_full, nd[0])
            at["values"] = nd[0]
            pe.wait_ge(rows_act, 2)
            pe.wait_ge(rows_dve, 2)
            bk = bank_d()
            for t in range(NT):
                r = rows_of(t)
                nc.tensor.transpose(bk[0:r, 4 * t:4 * t + 4], irow[:, t * TR:t * TR + r], ident[0:4, 0:4])
                nc.tensor.transpose(bk[0:r, 20 + 4 * t:24 + 4 * t], trow[:, t * TR:t * TR + r], ident[0:4, 0:4])
            nc.tensor.transpose(bk[0:NS, 40:44], irow[:, NP_:NTOK], ident[0:4, 0:4])
            nc.tensor.transpose(bk[0:NS, 44:48], frow[:, NP_:NTOK], ident[0:4, 0:4]).then_inc(dve_full, 1)
            at["gcol"] = nd[0]
            pe.wait_ge(act_free, qk_groups)
            for src in (qT, kT):
                bk = bank_d()
                for h in range(H):
                    last = nc.tensor.transpose(bk[0:NS, h * 128:h * 128 + 128], src[:, h, NP_:NTOK], ident)
                last.then_inc(dve_full, 1)
            pe.wait_ge(dve_free, at["values"])
            bk = bank_d()
            for h in range(H):
                last = nc.tensor.transpose(bk[:, h * NS:h * NS + NS], vsn[:, h * 128:h * 128 + 128], ident[0:NS, 0:NS])
            last.then_inc(dve_full, 1)

            offs = [0]
            for t in range(NT):
                offs.append(offs[-1] + NP_ - t * TR)

            def scores(h):
                if h >= 2:
                    pe.wait_ge(wexp_done, NT * (h - 1))
                mm(MBANK[h % 2][:, :], ident[0:4, h:h + 1].broadcast_to([4, 128]), mrow[:, 0:NP_], start=True, stop=True).then_inc(mb_full, 1)
                for t in range(NT):
                    r = rows_of(t)
                    bk = bank_d()
                    mm(bk[0:r, 0:NP_ - t * TR], kT[:, h, t * TR:t * TR + r], qT[:, h, t * TR:NP_], start=True, stop=True).then_inc(dve_full, 1)
                    at["scores", h, t] = nd[0]
                bk = bank_d()
                for t in range(4):
                    last = nc.tensor.transpose(bk[0:TR, t * 128:t * 128 + 128], kT[:, h, t * TR:t * TR + TR], ident)
                last.then_inc(dve_full, 1)
                bk = bank_d()
                nc.tensor.transpose(bk[0:LAST, 0:128], kT[:, h, 4 * TR:NP_], ident).then_inc(dve_full, 1)
                at["keys", h] = nd[0]

            def numerators(h):
                for j in range(NT):
                    pe.wait_ge(sel_done, NT * h + j + 1)
                    bk = bank_a()
                    nj = rows_of(j)
                    for i in range(j + 1):
                        ni = rows_of(i)
                        c0 = offs[i] + (j - i) * TR
                        last = mm(bk[0:nj, 0:HD + 1], pst[0:ni, c0:c0 + nj], vn[0:ni, i, h, :], start=(i == 0), stop=(i == j))
                    last.then_inc(act_full, 1)
                at["numerators", h] = na[0]

            def state(h):
                pe.wait_ge(dve_free, at["keys", h])
                bk = bank_d()
                for i in range(NT):
                    ni = rows_of(i)
                    mm(bk[:, 0:HD], vn[0:ni, i, h, 0:HD], kw[0:ni, i, :], start=(i == 0), stop=(i == NT - 1))
                for i in range(NT):
                    ni = rows_of(i)
                    last = mm(bk[0:1, HD:2 * HD], vn[0:ni, i, h, HD:HD + 1], kw[0:ni, i, :], start=(i == 0), stop=(i == NT - 1))
                last.then_inc(dve_full, 1)
                at["state", h] = nd[0]

            def transpose_heads(h, bk=None):
                pe.wait_ge(hn_ready, h + 1)
                bk = bk or bank_d()
                for t in range(NT):
                    r = rows_of(t)
                    last = nc.tensor.transpose(bk[:, t * TR:t * TR + r], hn[0:r, h % 2, t, 0:HD], ident[0:r, 0:r])
                last.then_inc(dve_full, 1)
                at.setdefault(("heads", h), nd[0])

            def transpose_last(i):
                pe.wait_ge(act_free, at["u", i])
                bk = bank_d()
                for g in range(2):
                    last = nc.tensor.transpose(bk[0:NPOOL + NS, g * 128:g * 128 + 128], uT[:, 2 * i + g, PADC + NP_ - NPOOL:PADC + NTOK], ident)
                last.then_inc(dve_full, 1)
                at["last u", i] = nd[0]

            pe.wait_ge(memset_done, 1)
            scores(0)
            project("og", (0, 1))
            at["og", 0] = na[0]
            numerators(0)
            state(0)
            scores(1)
            project("og", (2, 3))
            at["og", 1] = na[0]
            transpose_heads(0)
            numerators(1)
            state(1)
            scores(2)
            project("u", (0, 1))
            at["u", 0] = na[0]
            transpose_heads(1)
            transpose_last(0)
            numerators(2)
            state(2)
            scores(3)
            project("u", (2, 3))
            at["u", 1] = na[0]
            transpose_heads(2)
            transpose_last(1)
            numerators(3)
            state(3)
            for g in range(4):
                pe.wait_ge(dif_done, g + 1)
                for c0, cn in GRP:
                    bk = bank_a()
                    mm(bk[:, 0:cn], poolw[:, g, :], uT[:, g, PADC + c0:PADC + c0 + cn], start=True, stop=True).then_inc(act_full, 1)
            at["pool"] = na[0]

            def rows_project(t, names, src):
                for name in names:
                    w = use_block(name)
                    bk = bank_d()
                    contract(bk[0:TR, :], lambda k: src[:, k, t * TR:t * TR + TR], lambda k: w[:, k, :]).then_inc(dve_full, 1)
                    used[BI[name]] = (dve_full, nd[0])

            WO = ("wo0", "wo1")
            pe.wait_ge(act_free, na[0])
            pe.wait_ge(dve_free, nd[0])
            head_bank = bank_d()
            at["heads", 3] = nd[0]
            banks = []
            for name in WO:
                banks.append(bank_d())
                w = use_block(name)
                for k in range(KC - 1):
                    mm(banks[-1][0:TR, :], mixT[:, k, 0:TR], w[:, k, :], start=(k == 0), stop=False)
                if name == "wo0":
                    transpose_heads(3, head_bank)
            pe.wait_ge(dve_free, at["heads", 3])
            for name, bk in zip(WO, banks):
                w = wring[:, BI[name] % WR]
                mm(bk[0:TR, :], mixT[:, KC - 1, 0:TR], w[:, KC - 1, :], start=False, stop=True).then_inc(dve_full, 1)
            rows_project(1, WO, mixT)
            transpose_x(0, x1_ready)
            pe.wait_ge(cq_done, NS)
            bk = bank_d()
            for h in range(H):
                last = nc.tensor.transpose(bk[0:NS, h * 128:h * 128 + 128], cq[:, h, :], ident)
            last.then_inc(dve_full, 1)
            rows_project(2, WO, mixT)
            transpose_x(1, x1_ready)
            pe.wait_ge(hs_ready, 1)
            bk = bank_d()
            for h in range(H):
                last = nc.tensor.transpose(bk[:, h * NS:h * NS + NS], vsn[:, h * 128:h * 128 + 128], ident[0:NS, 0:NS])
            last.then_inc(dve_full, 1)
            samples_mixed = nd[0]
            rows_project(3, WO, mixT)
            transpose_x(2, x1_ready)
            pe.wait_ge(dve_free, samples_mixed)
            rows_project(4, WO, mixT)
            transpose_x(3, x1_ready)

            project("wq0", range(4), groups=GRP[0:1])
            transpose_x(4, x1_ready)
            pe.wait_ge(act_free, na[0])
            project("wq0", range(4), groups=GRP[1:2])
            project("wq1", range(4), groups=GRP[1:2])
            pe.wait_ge(act_free, na[0])
            for q in range(2):
                bk = bank_a()
                for k in range(4):
                    last = nc.tensor.transpose(bk[0:NS, k * 128:k * 128 + 128], qcT[:, 4 * q + k, NP_:NTOK], ident)
                last.then_inc(act_full, 1)
            at["sample q"] = na[0]
            project("wq1", range(4), groups=GRP[0:1])
            pe.wait_ge(act_free, na[0])

            NQ = NT * 4

            def attend(n):
                t, h = divmod(n, 4)
                bk = bank_a()
                for k in range(2):
                    last = mm(bk[0:TR, 0:NM], qcT[:, 2 * h + k, t * TR:t * TR + TR], mkT[:, 2 * h + k, :], start=(k == 0), stop=(k == 1))
                last.then_inc(act_full, 1)
                at["attend", n] = na[0]

            def transpose_probs(n):
                pe.wait_ge(prob_ready, n + 1)
                bk = bank_a()
                for m in range(2):
                    last = nc.tensor.transpose(bk[:, m * TR:m * TR + TR], Er[0:TR, n % 4, m * 128:m * 128 + 128], ident[0:TR, 0:TR])
                last.then_inc(act_full, 1)
                at["probs", n] = na[0]

            def context(h, ec, group):
                c0, cn = group
                bk = bank_a()
                for m in range(2):
                    last = mm(bk[:, 0:cn], mv[:, m, h * CE + ec * 128:h * CE + ec * 128 + 128], paT[:, h, m, c0:c0 + cn], start=(m == 0), stop=(m == 1))
                last.then_inc(act_full, 1)

            for n in range(NQ):
                attend(n)
                if n >= 3:
                    transpose_probs(n - 3)
                if n >= 16:
                    pe.wait_ge(act_free, at["probs", 11])
                    for g in (2 * (n - 16), 2 * (n - 16) + 1):
                        context(g // 2, g % 2, GRP[0])
            for n in range(NQ - 3, NQ):
                transpose_probs(n)
            pe.wait_ge(k_used, NS)
            bk = bank_d()
            for m in range(2):
                last = nc.tensor.transpose(bk[0:32, m * 128:m * 128 + 128], sS[:, m, :], ident)
            last.then_inc(dve_full, 1)
            at["sample scores"] = nd[0]
            pe.wait_ge(act_free, at["probs", NQ - 1])
            for g in range(8):
                context(g // 2, g % 2, GRP[1])
            pe.wait_ge(s_prob, 1)
            bk = bank_d()
            for m in range(2):
                last = nc.tensor.transpose(bk[:, m * 32:m * 32 + 32], Es[:, m * 128:m * 128 + 128], ident[0:32, 0:32])
            last.then_inc(dve_full, 1)
            pe.wait_ge(dve_free, nd[0])
            bk = bank_d()
            for b in range(NS):
                n = NS + b
                pe.wait_ge(kv_in[n % 3], 16 * (n // 3 + 1))
                for h in range(4):
                    for m in range(2):
                        last = mm(bk[0:32, 0:CE], paz[:, m, 4 * b + h, :], kvr[:, n % 3, m, h * CE:h * CE + CE],
                                  start=(b + h + m == 0), stop=(b == NS - 1 and h == 3 and m == 1))
                if b < NS - 1:
                    last.then_inc(v_used, 1)
            last.then_inc(dve_full, 1)
            at["sample context"] = nd[0]
            pe.wait_ge(dve_free, nd[0])
            bk = bank_d()
            for ec in range(2):
                last = nc.tensor.transpose(bk[:, ec * 32:ec * 32 + 32], ctxs[:, ec * 128:ec * 128 + 128], ident[0:32, 0:32])
            last.then_inc(dve_full, 1)

            def router(t):
                bk = bank_a()
                contract(bk[0:20, 0:TR], lambda k: wr[:, k, :], lambda k: xT[:, k, t * TR:t * TR + TR]).then_inc(act_full, 1)
                at["router", t] = na[0]

            def router_rows(t):
                pe.wait_ge(act_free, at["router", t])
                bk = bank_d()
                nc.tensor.transpose(bk[0:TR, 0:20], lgT[:, t % 2, :], ident[0:20, 0:20]).then_inc(dve_full, 1)
                at["router rows", t] = nd[0]

            def count_choices(n):
                a0, a1 = ROUTED[n]
                pe.wait_ge(mask_ready, n + 1)
                bk = bank_d()
                for t in range(a0, a1 + (a1 == NT)):
                    for i in range(min(t + 1, NT)):
                        last = mm(bk[0:TR, t * NE:t * NE + NE], (trib if i == t else onesb)[:, :], Mb16[:, i, :],
                                  start=(i == 0), stop=(i == min(t, NT - 1)))
                last.then_inc(dve_full, 1)

            pe.wait_ge(act_free, na[0])
            pe.wait_ge(dve_free, nd[0])
            WC = ("wc0", "wc1")
            for t in range(NT):
                rows_project(t, WC[0:1], ctxT)
                if t >= 2:
                    router_rows(t - 2)
                if t >= 1:
                    transpose_x(t - 1, x2_ready)
                rows_project(t, WC[1:2], ctxT)
                if t >= 1:
                    pe.wait_ge(act_free, na[0])
                    router(t - 1)
            count_choices(0)
            router_rows(NT - 2)
            transpose_x(NT - 1, x2_ready)
            pe.wait_ge(act_free, na[0])
            router(NT - 1)
            count_choices(1)
            router_rows(NT - 1)
            count_choices(2)

            pe.wait_ge(dve_free, nd[0])

            GU = [ps[2], ps[3], ps[6]]
            YB = [ps[4], ps[5]]

            def turn_rows(e, s, k):
                if not (isinstance(e, int) and e == 0):
                    pe.wait_ge(xgT_act, e)
                    pe.wait_ge(xgT_dve, e)
                pe.wait_ge(xg_in[s], k * 16 + 16)
                for q in range(2):
                    for j in range(4):
                        kk = 4 * q + j
                        last = nc.tensor.transpose(ps[q][:, j * C:j * C + C], xg[:, s, kk * 128:kk * 128 + 128], ident)
                    last.then_inc(xgT_full, 1)

            def gate_up(e, s, k):
                pe.wait_ge(blk_in[s], k * 32 + (16 * (NB // WR) + 32))
                pe.wait_ge(xgT_act, e + 1)
                pe.wait_ge(xgT_dve, e + 1)
                for f in range(4):
                    last = contract(GU[s][:, f * C:f * C + C], lambda kk: wring[:, s, kk, f * 128:f * 128 + 128],
                                    lambda kk: xgT[:, s, kk, :])
                last.then_inc(gu_full, 1)

            def down(e, s, k, first=False):
                pe.wait_ge(dn_in[s], k * 16 + 16)
                pe.wait_ge(hh_ready, e + 1)
                if not first:
                    pe.wait_ge(y_act, e)
                    pe.wait_ge(y_dve, e)
                for q in range(2):
                    for f in range(2):
                        last = mm(YB[q][:, :], hh[:, s, f, :], dnr[:, s, f, q * 512:q * 512 + 512], start=(f == 0), stop=(f == 1))
                last.then_inc(y_full, 1)

            turn_rows(0, 0, 0)
            gate_up(0, 0, 0)
            turn_rows(1, 1, 0)
            gate_up(1, 1, 0)
            turn_rows(2, 2, 0)
            down(0, 0, 0, first=True)

            def expert_step(e, u, i):
                nxt, prv = (u + 1) % 3, (u + 2) % 3
                gate_up(e, u, i)
                turn_rows(e + 1, nxt, i + (1 if u == 2 else 0))
                down(e - 1, prv, i - (1 if u == 0 else 0))

            for e in (2, 3):
                expert_step(e, e % 3, e // 3)
            with pe.Fori(1, 4) as i:
                for u in range(1, 4):
                    expert_step(i * 3 + u, u % 3, i + u // 3)
            for e in (13, 14):
                expert_step(e, e % 3, e // 3)
            gate_up(15, 0, 5)
            down(14, 2, 4)
            down(15, 0, 5)

            pe.wait_ge(flag_ready, 1)
            over = pe.value_load(flag[0:1, 0:1], min_val=0, max_val=1)
            with pe.If(over > 0):
                with pe.Fori(0, NE) as e:
                    pe.wait_ge(ov_w, e * 48 + 48)
                    for c in range(1, NCH):
                        n = e * (NCH - 1) + (c - 1)
                        pe.wait_ge(ov_x, n * 16 + 16)
                        for q in range(2):
                            for j in range(4):
                                kk = 4 * q + j
                                last = nc.tensor.transpose(ps[q][:, j * C:j * C + C], xg[:, 0, kk * 128:kk * 128 + 128], ident)
                        last.then_inc(ov_t, 1)
                        pe.wait_ge(ov_tc, n + 1)
                        for f in range(4):
                            last = contract(GU[0][:, f * C:f * C + C], lambda kk: wring[:, 0, kk, f * 128:f * 128 + 128],
                                            lambda kk: xgT[:, 0, kk, :])
                        last.then_inc(ov_gu, 1)
                        pe.wait_ge(ov_h, n + 1)
                        for q in range(2):
                            for f in range(2):
                                last = mm(YB[q][:, :], hh[:, 0, f, :], dnr[:, 0, f, q * 512:q * 512 + 512], start=(f == 0), stop=(f == 1))
                        last.then_inc(ov_y, 1)

        @block.sync
        def _(sp):
            def block_load(i):
                if i >= WR:
                    sp.wait_ge(*used[i - WR])
                sp.dma_start(wring[:, i % WR], BLOCKS[i][1]).then_inc(blk_in[i % WR], 16)

            def kv_load(n):
                if n >= 3:
                    if n - 3 < NS:
                        sp.wait_ge(k_used, n - 2)
                    else:
                        sp.wait_ge(v_used, n - 3 - NS + 1)
                sp.dma_start(kvr[:, n % 3], kv_src[n].rearrange("(m p) h e -> p m (h e)", p=128)).then_inc(kv_in[n % 3], 16)

            def expert_load(e, s):
                sp.dma_start(wring[:, s, :, 0:DE], one_expert(gate_w, e)).then_inc(blk_in[s], 16)
                sp.dma_start(wring[:, s, :, DE:2 * DE], one_expert(up_w, e)).then_inc(blk_in[s], 16)

            def down_load(e, s):
                sp.dma_start(dnr[:, s], one_expert(down_w, e)).then_inc(dn_in[s], 16)

            for m in range(2):
                sp.dma_start(memn[:, m, :], a["mem_prompt"][0, m * 128:m * 128 + 128, :]).then_inc(mem_in[m], 16)
            sp.dma_start(wring[:, 0, 0:4, :], BLOCKS[0][1][:, 0:4, :]).then_inc(half_in, 16)
            sp.dma_start(wring[:, 0, 4:KC, :], BLOCKS[0][1][:, 4:KC, :]).then_inc(blk_in[0], 16)
            for i in range(1, BI["wc0"] + 1):
                block_load(i)
            sp.wait_ge(act_full, at["pool"])
            for n in range(3):
                kv_load(n)
            block_load(BI["wc1"])
            sp.wait_ge(sq2_out, 16)
            for i in range(2):
                sp.wait_ge(c_store[i], 16 * BUF.count(i))
            for b in range(NS):
                for hf in range(2):
                    if b >= 1:
                        sp.wait_ge(kq_done, 2 * (b - 1) + hf + 1)
                    sp.dma_start(qb[:, hf * 512:hf * 512 + 512], sq2_d[b, hf * 512:hf * 512 + 512].partition_broadcast(128)).then_inc(qb_in[hf], 16)
                if b >= 2:
                    kv_load(b + 1)
            sp.wait_ge(*used[NB - WR])
            expert_load(0, 0)
            for n in range(NS + 1, 2 * NS):
                kv_load(n)
            sp.wait_ge(dve_full, at["sample context"])
            for e in range(3):
                down_load(e, e)
            for e in (1, 2):
                sp.wait_ge(*used[NB - WR + e])
                expert_load(e, e)

            def refill(e, s):
                sp.wait_ge(gu_full, e - 2)
                expert_load(e, s)
                sp.wait_ge(y_full, e - 2)
                down_load(e, s)

            with sp.Fori(0, 4) as i:
                for u in range(3):
                    refill(i * 3 + (3 + u), u)
            refill(NE - 1, (NE - 1) % 3)

            sp.wait_ge(flag_ready, 1)
            over = sp.value_load(flag[0:1, 0:1], min_val=0, max_val=1)
            with sp.If(over > 0):
                sp.wait_ge(gu_full, NE)
                sp.wait_ge(lst_out, 16 * 2 * NT)
                sp.wait_ge(y_full, NE)
                with sp.Fori(0, NE) as e:
                    sp.dma_start(wring[:, 0, :, 0:DE], one_expert(gate_w, e)).then_inc(ov_w, 16)
                    sp.dma_start(wring[:, 0, :, DE:2 * DE], one_expert(up_w, e)).then_inc(ov_w, 16)
                    sp.dma_start(dnr[:, 0], one_expert(down_w, e)).then_inc(ov_w, 16)
                    for c in range(1, NCH):
                        n = e * (NCH - 1) + (c - 1)
                        sp.dma_start(list1.bitcast(U32).unsqueeze(1), lst_e[c * C:c * C + C, bass.ds(e, 1), :]).then_inc(ov_idx, 16)
                        sp.wait_ge(ov_turn, n + 1)
                        sp.wait_ge(ov_yc, n + 1)
                        sp.dma_start(y_e[c * C:c * C + C, bass.ds(e, 1), :], ysb[:, 0:1]).then_inc(ov_out, 16)
            for t in range(NT):
                if t < NT - 1:
                    sp.wait_ge(x3_ready, t + 1)
                else:
                    sp.wait_ge(x4_ready, 1)
                sp.dma_start(o_xp[0, t * TR:t * TR + rows_of(t), :], xn[0:rows_of(t), t, :]).then_inc(x_out, 16)
            sp.dma_start(o_xs.rearrange("b one d -> (b one) d"), xn[LAST:TR, NT - 1, :]).then_inc(x_out, 16)
            sp.wait_ge(x_out, 16 * (NT + 1))
            sp.wait_ge(out_done, 16 * 2)
            for i in range(2):
                sp.wait_ge(c_store[i], 16 * BUF.count(i))
            for i in range(2):
                sp.wait_ge(c_out[i], 64)
            sp.wait_ge(mk_out, 64)
            sp.wait_ge(mv_out, 64)
            sp.wait_ge(un_out, 48)
            sp.wait_ge(sn_out, 16)

        @block.scalar
        def _(act):
            nf = [0]
            steps = [0]
            A = nc.scalar.activation

            def full():
                k = nf[0]
                nf[0] += 1
                act.wait_ge(act_full, k + 1)
                return RING_A[k % 3]

            def link(ins):
                steps[0] += 1
                ins.then_inc(act_step, 1)
                act.wait_ge(act_step, steps[0])

            act.dma_start(con[:, :], a["consts"]).then_inc(con_in, 16)
            for m in range(2):
                for q in range(2):
                    bk = full()
                    A(memT[:, 4 * q:4 * q + 4, m * 128:m * 128 + 128], bk[:, :].rearrange("p (k c) -> p k c", k=4), ACT.Copy).then_inc(act_free, 1)
            xp = a["x_prompt"][0]
            for t in range(NT):
                act.dma_start(xn[0:rows_of(t), t, :], xp[t * TR:t * TR + rows_of(t), :]).then_inc(x_in, 16)
            act.dma_start(xn[LAST:TR, NT - 1, :], a["x_sample"][:, 0, :]).then_inc(x_in, 16)
            act.dma_start(gb[:, 0, :], a["emb_ln_g"].partition_broadcast(128)).then_inc(emb_in, 16)
            act.dma_start(gb[:, 1, :], a["emb_ln_b"].partition_broadcast(128)).then_inc(emb_in, 16)
            act.dma_start(cache, a["cache_pool"][0].rearrange("b r c -> (b r) c")).then_inc(cache_in, 16)
            for name, dstn in (("k", mkn), ("v", mv)):
                for hf in range(2):
                    for m in range(2):
                        bk = full()
                        A(dstn[:, m, hf * 512:hf * 512 + 512], bk[:, :], ACT.Copy).then_inc(act_free, 1)
                        act.wait_ge(act_free, nf[0])
                        out = (o_pmk if name == "k" else o_pmv)[0, 0].rearrange("(m p) h e -> p m (h e)", p=128)
                        act.dma_start(out[:, m, hf * 512:hf * 512 + 512], dstn[:, m, hf * 512:hf * 512 + 512]).then_inc(mk_out if name == "k" else mv_out, 16)
            for m in range(2):
                for q in range(2):
                    bk = full()
                    A(mkT[:, 4 * q:4 * q + 4, m * 128:m * 128 + 128], bk[:, :].rearrange("p (k c) -> p k c", k=4), ACT.Copy).then_inc(act_free, 1)

            def take_x(t):
                for q in range(2):
                    bk = full()
                    A(xT[:, 4 * q:4 * q + 4, t * TR:t * TR + TR], bk[:, 0:4 * TR].rearrange("p (k c) -> p k c", k=4), ACT.Copy).then_inc(act_free, 1)

            for t in range(NT):
                take_x(t)
            act.wait_ge(small_in, 16 * 13)
            act.wait_ge(mk_out, 64)
            for c0, cn in GRP:
                bk = full()
                A(irow[:, c0:c0 + cn], bk[0:4, 0:cn], ACT.Identity, bias=colv[0:4, 8:9])
                A(frow[:, c0:c0 + cn], bk[32:36, 0:cn], ACT.Identity, bias=colv[32:36, 9:10]).then_inc(act_free, 1)
            act.wait_ge(act_free, nf[0])
            link(A(trow, frow, ACT.Abs))
            link(A(trow, trow, ACT.Exp, scale=-1.0))
            A(trow, trow, ACT.Ln, bias=1.0).then_inc(rows_act, 1)

            def take_projection(dstn, cts, scale, groups=GRP, off=0):
                for ct in cts:
                    for c0, cn in groups:
                        bk = full()
                        A(dstn[:, ct, off + c0:off + c0 + cn], bk[:, 0:cn], ACT.Copy, scale=scale).then_inc(act_free, 1)

            take_projection(qT, range(4), HD ** -0.5)
            act.wait_ge(rows_dve, 1)
            A(trow[:, 0:NP_], trow[:, 0:NP_], ACT.Exp, scale=-1.0).then_inc(rows_act, 1)
            take_projection(kT, range(4), 1.0)

            offs = [0]
            for t in range(NT):
                offs.append(offs[-1] + NP_ - t * TR)

            def weights(h):
                act.wait_ge(mb_full, h + 1)
                mb = MBANK[h % 2]
                act.wait_ge(dve_free, at["gcol"])
                for t in range(NT):
                    r = rows_of(t)
                    bias = gcol[0:r, 4 * t + h:4 * t + h + 1]
                    A(wcol[0:r, t, h:h + 1], mb[0:r, NP_ - 1:NP_], ACT.Exp, bias=bias)
                    ins = A(pst[0:r, offs[t]:offs[t + 1]], mb[0:r, t * TR:NP_], ACT.Exp, bias=bias)
                    ins.then_inc(wexp_done, 1)

            def take_numerators(h):
                if h >= 2:
                    act.wait_ge(dve_full, at["heads", h - 2])
                for j in range(NT):
                    bk = full()
                    r = rows_of(j)
                    A(hn[0:r, h % 2, j, :], bk[0:r, 0:HD + 1], ACT.Copy).then_inc(act_free, 1)

            def take_og(cts):
                for ct in cts:
                    for c0, cn in GRP:
                        bk = full()
                        A(sgT[:, ct, c0:c0 + cn], bk[:, 0:cn], ACT.Exp, scale=-1.0).then_inc(act_free, 1)

            def finish_og(cts):
                act.wait_ge(act_free, nf[0])
                x = sgT[:, cts[0]:cts[1] + 1, :]
                link(A(x, x, ACT.Ln, bias=1.0))
                A(x, x, ACT.Exp, scale=-1.0).then_inc(sig_done, 1)

            weights(0)
            act.wait_ge(sgate_dif, 1)
            A(sg8[:, 12:20], sg8[:, 12:20], ACT.Exp)
            A(sg8[:, 20:24], sg8[:, 8:12], ACT.Exp, scale=-1.0).then_inc(sgate_exp, 1)
            take_og((0, 1))
            take_numerators(0)
            finish_og((0, 1))
            weights(1)
            take_og((2, 3))
            take_numerators(1)
            finish_og((2, 3))
            weights(2)
            take_projection(uT, (0, 1), 1.0, off=PADC)
            take_numerators(2)
            weights(3)
            take_projection(uT, (2, 3), 1.0, off=PADC)
            take_numerators(3)
            act.wait_ge(c_store[0], 16 * BUF.count(0))
            for g in range(4):
                for c0, cn in GRP:
                    bk = full()
                    A(mixT[:, g, c0:c0 + cn], bk[:, 0:cn], ACT.Copy, scale=colv[:, g:g + 1]).then_inc(act_free, 1)
            for t in range(4):
                take_x(t)
            def take_queries(b, groups):
                take_projection(qcT[:, 4 * b:4 * b + 4, :], range(4), CE ** -0.5, groups=groups)

            take_queries(0, GRP[0:1])
            take_x(4)
            take_queries(0, GRP[1:2])
            take_queries(1, GRP[1:2])
            act.wait_ge(un_out, 48)
            for q in range(2):
                bk = full()
                A(qs2[:, q * 512:q * 512 + 512], bk[0:NS, :], ACT.Copy).then_inc(act_free, 1)
            take_queries(1, GRP[0:1])

            def take_context(h, ec, group, samples):
                c0, cn = group
                bk = full()
                cn -= samples
                A(ctxT[:, 2 * h + ec, c0:c0 + cn], bk[:, 0:cn], ACT.Copy).then_inc(act_free, 1)

            def take_probs(n):
                t, h = divmod(n, 4)
                bk = full()
                A(paT[:, h, :, t * TR:t * TR + TR], bk[:, 0:2 * TR].rearrange("p (m c) -> p m c", m=2), ACT.Copy).then_inc(act_free, 1)

            NQ = NT * 4
            act.wait_ge(c_store[1], 16 * BUF.count(1))
            for n in range(NQ):
                bk = full()
                act.wait_ge(nmax_done, n + 1)
                A(Er[0:TR, n % 4, :], bk[0:TR, 0:NM], ACT.Exp, bias=mx4[0:TR, n % 4:n % 4 + 1], accum_out=mx4[0:TR, 4 + n % 4:5 + n % 4]).then_inc(act_free, 1)
                if n >= 3:
                    take_probs(n - 3)
                if n >= 16:
                    for g in (2 * (n - 16), 2 * (n - 16) + 1):
                        take_context(g // 2, g % 2, GRP[0], 0)
            for n in range(NQ - 3, NQ):
                take_probs(n)
            for g in range(4):
                take_context(g // 2, g % 2, GRP[1], NS)
            act.wait_ge(s_nmax, 1)
            A(Es, RING_D[(at["sample scores"] - 1) % 3][0:32, 0:NM], ACT.Exp, bias=mx4[0:32, 0:1], accum_out=mx4[0:32, 4:5]).then_inc(s_exp, 1)
            for g in range(4, 8):
                take_context(g // 2, g % 2, GRP[1], NS)

            def take_router(t):
                bk = full()
                if t >= 2:
                    act.wait_ge(dve_full, at["router rows", t - 2])
                A(lgT[:, t % 2, :], bk[0:20, 0:TR], ACT.Identity, bias=colv[0:20, 10:11]).then_inc(act_free, 1)

            def route_exp(n):
                r = rt[:, ROUTED[n][0]:ROUTED[n][1], :]
                for i, x in enumerate((r[:, :, 20:24], r[:, :, 93:94])):
                    act.wait_ge(rt_dve, 2 * n + i + 1)
                    A(x, x, ACT.Exp).then_inc(rt_act, 1)

            for t in range(NT):
                if t == NT - 1:
                    route_exp(0)
                take_x(t)
                take_router(t)
            route_exp(1)
            route_exp(2)
            act.wait_ge(x2_out, 16 * NT)
            for t in range(NT):
                A(xn[0:TR, t, :], xn[0:TR, t, :], ACT.Copy, scale=ALPHA).then_inc(xa_ready, 1)

            GU = [ps[2], ps[3], ps[6]]

            def expert_in(e, s):
                act.wait_ge(xgT_full, e * 2 + 1)
                A(xgT[:, s, 0:4, :], ps[0][:, :].rearrange("p (k c) -> p k c", k=4), ACT.Copy).then_inc(xgT_act, 1)

            def expert_exp(e, s):
                act.wait_ge(gu_full, e + 1)
                if not (isinstance(e, int) and e < 1):
                    act.wait_ge(hh_ready, e)
                A(sgm[:, 0, :], GU[s][:, 0:2 * C], ACT.Exp, scale=-1.0).then_inc(sgm_ready, 1)

            def expert_out(e, s, k):
                act.wait_ge(y_full, e + 1)
                if not (isinstance(k, int) and k == 0):
                    act.wait_ge(y_out[s], k * 16)
                act.wait_ge(gate_set, e + 1)
                A(ysb[:, s, 0:512], ps[4][:, :], ACT.Copy, scale=gate3[:, s:s + 1]).then_inc(y_act, 1)
                act.wait_ge(y_act, e + 1)
                act.wait_ge(y_dve, e + 1)
                act.dma_start(y_e[0:C, bass.ds(e, 1), :], ysb[:, s:s + 1]).then_inc(y_out[s], 16)

            expert_in(0, 0)
            expert_in(1, 1)
            expert_exp(0, 0)
            expert_exp(1, 1)
            expert_in(2, 2)
            expert_out(0, 0, 0)

            def expert_step(e, u, i):
                expert_exp(e, u)
                expert_in(e + 1, (u + 1) % 3)
                expert_out(e - 1, (u + 2) % 3, i - (1 if u == 0 else 0))

            for e in (2, 3):
                expert_step(e, e % 3, e // 3)
            with act.Fori(1, 4) as i:
                for u in range(1, 4):
                    expert_step(i * 3 + u, u % 3, i + u // 3)
            for e in (13, 14):
                expert_step(e, e % 3, e // 3)
            expert_exp(15, 0)
            expert_out(14, 2, 4)
            expert_out(15, 0, 5)

            act.wait_ge(flag_ready, 1)
            over = act.value_load(flag[0:1, 0:1], min_val=0, max_val=1)
            with act.If(over > 0):
                act.wait_ge(y_out[0], 96)
                with act.Fori(0, NE * (NCH - 1)) as n:
                    act.wait_ge(ov_gu, n + 1)
                    A(sgm[:, 0, :], GU[0][:, 0:2 * C], ACT.Exp, scale=-1.0).then_inc(ov_sg, 1)
            for t in range(NT - 1):
                act.wait_ge(rstd_ready, 3 * NT + t + 1)
                act.wait_ge(x3_centred, t + 1)
                A(xn[0:TR, t, :], xn[0:TR, t, :], ACT.Copy, scale=rstd[0:TR, t:t + 1]).then_inc(x3_scaled, 1)

        @block.vector
        def _(dve):
            V = nc.vector
            nf = [0]
            steps = [0]

            def full():
                k = nf[0]
                nf[0] += 1
                dve.wait_ge(dve_full, k + 1)
                return RING_D[k % 3]

            def link(ins):
                steps[0] += 1
                ins.then_inc(dve_step, 1)
                dve.wait_ge(dve_step, steps[0])

            pows = [0]

            def statistics(t, q):
                return V.bn_stats(st[0:TR, 6 * q:6 * q + 6], xn[0:TR, t, q * 512:q * 512 + 512])

            def norm(t, signal, finish=True, first_known=False):
                if not first_known:
                    statistics(t, 0)
                link(statistics(t, 1))
                pows[0] += 1
                V.bn_aggr(agg[0:TR, :], st[0:TR, :]).then_inc(var_ready, 1)
                dve.wait_ge(var_ready, pows[0])
                centred = V.scalar_tensor_tensor(xn[0:TR, t, :], xn[0:TR, t, :], agg[0:TR, 0:1], gb[0:TR, 0, :], ALU.subtract, ALU.mult)
                if not finish:
                    centred.then_inc(signal, 1)
                    dve.wait_ge(rstd_ready, pows[0])
                    return
                link(centred)
                dve.wait_ge(rstd_ready, pows[0])
                V.scalar_tensor_tensor(xn[0:TR, t, :], xn[0:TR, t, :], rstd[0:TR, t:t + 1], gb[0:TR, 1, :], ALU.mult, ALU.add).then_inc(signal, 1)

            dve.wait_ge(x_in, 96)
            dve.wait_ge(emb_in, 32)
            for t in range(NT):
                norm(t, x0_ready)
            bk = full()
            cT = bk[:, 0:4 * NS * NPOOL].rearrange("p (g b r) -> p g b r", g=4, b=NS)
            for g in range(4):
                w = 2 << g
                last = V.tensor_reduce(csum[:, g, :], cT[:, g, :, NPOOL - (w - 1):NPOOL], AX, ALU.add)
            last.then_inc(dve_free, 1)
            dve.wait_ge(con_in, 16)
            V.tensor_copy(trib[:, :], con[0:TR, 128:128 + TR])

            dve.wait_ge(rows_act, 1)
            V.memset(zrow, 0.0)
            link(V.tensor_scalar(brow, frow, 0.0, None, ALU.min))
            link(V.tensor_tensor(frow, brow, trow, ALU.subtract))
            link(V.tensor_tensor_scan(brow[:, 0:NP_], frow[:, 0:NP_], zrow[:, 0:NP_], 0.0, ALU.add, ALU.add))
            link(V.tensor_tensor(irow[:, 0:NP_], irow[:, 0:NP_], brow[:, 0:NP_], ALU.subtract))
            link(V.tensor_tensor_scan(mrow[:, 0:NP_], irow[:, 0:NP_], irow[:, 0:NP_], 0.0, ALU.max, ALU.max))
            link(V.tensor_tensor(trow[:, 0:NP_], brow[:, 0:NP_], mrow[:, 0:NP_], ALU.add))
            V.tensor_copy(colv[0:4, 11:12], trow[:, NP_ - 1:NP_]).then_inc(rows_dve, 1)
            V.tensor_scalar(mrow[:, 0:NP_], mrow[:, 0:NP_], -1.0, None, ALU.mult).then_inc(rows_dve, 1)

            for t in range(NT):
                bk = full()
                src = bk[0:TR, :].rearrange("p (h c) -> p h c", h=H)
                if t == NT - 1:
                    V.tensor_copy(vsn, bk[LAST:TR, :])
                V.tensor_copy(vn[0:TR, t, :, 0:HD], src).then_inc(dve_free, 1)
            bk = full()
            dve.wait_ge(memset_done, 1)
            for t in range(NT):
                r = rows_of(t)
                V.tensor_copy(gcol[0:r, 4 * t:4 * t + 4], bk[0:r, 4 * t:4 * t + 4])
                V.tensor_copy(gcol[0:r, 20 + 4 * t:24 + 4 * t], bk[0:r, 20 + 4 * t:24 + 4 * t])
            V.tensor_copy(sg8[:, 0:8], bk[0:NS, 40:48]).then_inc(dve_free, 1)
            bk = full()
            V.tensor_copy(qsn, bk[0:NS, :]).then_inc(dve_free, 1)
            bk = full()
            V.tensor_copy(ksn, bk[0:NS, :]).then_inc(dve_free, 1)
            bk = full()
            V.tensor_copy(vsT[:, :, :], bk[:, 0:H * NS].rearrange("p (h b) -> p h b", h=H)).then_inc(dve_free, 1)
            dve.wait_ge(dve_free, nf[0])
            dve.wait_ge(st_in, 32)
            link(V.tensor_tensor(sg8[:, 24:28], sg8[:, 4:8], sg8[:, 28:32], ALU.add))
            link(V.tensor_tensor(sg8[:, 8:12], sg8[:, 24:28], sg8[:, 0:4], ALU.max))
            link(V.tensor_tensor(sg8[:, 12:16], sg8[:, 0:4], sg8[:, 8:12], ALU.subtract))
            V.tensor_tensor(sg8[:, 16:20], sg8[:, 24:28], sg8[:, 8:12], ALU.subtract).then_inc(sgate_dif, 1)
            offs = [0]
            for t in range(NT):
                offs.append(offs[-1] + NP_ - t * TR)

            def products(h):
                for t in range(NT):
                    r = rows_of(t)
                    bk = full()
                    dve.wait_ge(wexp_done, NT * h + t + 1)
                    blk = pst[0:r, offs[t]:offs[t + 1]]
                    V.tensor_tensor(blk, bk[0:r, 0:NP_ - t * TR], blk, ALU.mult).then_inc(dve_free, 1)
                for q in range(2):
                    bk = full()
                    for t in (range(4) if q == 0 else (4,)):
                        r = rows_of(t)
                        last = V.tensor_scalar(kw[0:r, t, :], bk[0:r, (t % 4) * 128:(t % 4) * 128 + 128], wcol[0:r, t, h:h + 1], None, ALU.mult)
                    last.then_inc(dve_free, 1)

            products(0)
            dve.wait_ge(sgate_exp, 1)
            dve.wait_ge(dve_free, nf[0])
            v4 = lambda x: x.rearrange("p (h c) -> p h c", h=H)
            b4 = lambda x: x.unsqueeze(2).broadcast_to([NS, H, HD])
            pr = P[0:NS, 14830:14830 + 512]
            link(V.tensor_tensor(pr, qsn, ksn, ALU.mult))
            link(V.tensor_reduce(sg8[:, 32:36], v4(pr), AX, ALU.add))
            link(V.tensor_tensor(pr, qsn, n0, ALU.mult))
            link(V.tensor_reduce(sg8[:, 36:40], v4(pr), AX, ALU.add))
            link(V.tensor_tensor(sg8[:, 32:36], sg8[:, 32:36], sg8[:, 12:16], ALU.mult))
            link(V.tensor_tensor(sg8[:, 36:40], sg8[:, 36:40], sg8[:, 16:20], ALU.mult))
            link(V.tensor_tensor(sg8[:, 36:40], sg8[:, 36:40], sg8[:, 32:36], ALU.add))
            link(V.scalar_tensor_tensor(sg8[:, 40:44], sg8[:, 36:40], -1.0, sg8[:, 36:40], ALU.mult, ALU.max))
            link(V.tensor_tensor(sg8[:, 40:44], sg8[:, 40:44], sg8[:, 20:24], ALU.max))
            link(V.reciprocal(sg8[:, 40:44], sg8[:, 40:44]))
            link(V.tensor_tensor(v4(ksn), v4(ksn), b4(sg8[:, 12:16]), ALU.mult))
            link(V.tensor_tensor(v4(n0), v4(n0), b4(sg8[:, 16:20]), ALU.mult))
            V.tensor_tensor(n0, n0, ksn, ALU.add).then_inc(snat_ready, 1)
            link(V.tensor_tensor(v4(vsn), v4(vsn), b4(sg8[:, 32:36]), ALU.mult))

            def take_state(h):
                bk = full()
                if h >= 2:
                    dve.wait_ge(c_out[h % 2], 32)
                V.tensor_copy(Cout[:, h % 2, 0:HD], bk[:, 0:HD])
                V.tensor_copy(Cout[0:1, h % 2, HD:2 * HD], bk[0:1, HD:2 * HD]).then_inc(dve_free, 1)

            def head_norm1(h):
                dve.wait_ge(act_free, at["numerators", h])
                x = hn[0:TR, h % 2]
                qn = x[:, :, HD:HD + 1].rearrange("p t c -> p (t c)")
                d0 = den[0:TR, 0, :]
                link(V.scalar_tensor_tensor(d0, qn, -1.0, qn, ALU.mult, ALU.max))
                fl = gcol[0:TR, 20 + h:40:4]
                link(V.tensor_tensor(d0, d0, fl, ALU.max))
                link(V.reciprocal(d0, d0))
                link(V.tensor_tensor(x[:, :, 0:HD], x[:, :, 0:HD], d0.unsqueeze(2).broadcast_to([TR, NT, HD]), ALU.mult))
                for t in range(NT):
                    last = V.bn_stats(hst[0:TR, t, :], x[:, t, 0:HD])
                link(last)
                for t in range(NT):
                    last = V.bn_aggr(hagg[0:TR, t, :], hst[0:TR, t, :])
                last.then_inc(hs_var, 1)

            def head_norm2(h):
                dve.wait_ge(hs_rstd, h + 1)
                dve.wait_ge(hs_var, h + 1)
                for t in range(NT):
                    r = rows_of(t)
                    last = V.tensor_scalar(hn[0:r, h % 2, t, 0:HD], hn[0:r, h % 2, t, 0:HD], hagg[0:r, t, 0:1], den[0:r, 1, t:t + 1], ALU.subtract, ALU.mult)
                last.then_inc(hn_ready, 1)

            def take_heads(h):
                bk = full()
                dve.wait_ge(sig_done, h // 2 + 1)
                V.scalar_tensor_tensor(mixT[:, 4 + h, 0:NP_], bk[:, :], colv[:, 4 + h:5 + h], sgT[:, h, 0:NP_], ALU.mult, ALU.mult).then_inc(dve_free, 1)

            def carried(b):
                dve.wait_ge(c_in[BUF[b]], 32 * (earlier(b) + 1))
                for h in range(H):
                    last = V.tensor_tensor_reduce(out=Cq_b[BUF[b]][:, h, :], in0=Cs[BUF[b]][:, h, :], in1=Cq_b[BUF[b]][:, h, :], scale=1.0, scalar=0.0,
                                                  op0=ALU.mult, op1=ALU.add, accum_out=cq[:, h, b:b + 1])
                last.then_inc(cq_done, 1)

            def take_last(i):
                bk = full()
                V.tensor_copy(un[0:NPOOL + NS, 256 * i:256 * i + 256], bk[0:NPOOL + NS, 0:256]).then_inc(dve_free, 1)

            def pool_diff(g):
                w = 2 << g
                if g < 2:
                    dve.wait_ge(usum_done, g + 1)
                else:
                    dve.wait_ge(act_free, at["u", 1])
                    link(add_windows(V.tensor_tensor, g, link))
                s = pp[:, g % 2, PADC:PADC + NP_]
                u = uT[:, g, PADC:PADC + NP_]
                us = uT[:, g, PADC + NP_:PADC + NTOK]
                link(V.tensor_tensor(s[:, 0:16], s[:, 0:16], invc[:, g, :], ALU.mult))
                V.scalar_tensor_tensor(u[:, 16:], s[:, 16:], 1.0 / w, u[:, 16:], ALU.mult, ALU.subtract)
                V.tensor_tensor(u[:, 0:16], s[:, 0:16], u[:, 0:16], ALU.subtract)
                link(V.tensor_tensor(csum[:, g, :], csum[:, g, :], us, ALU.add))
                V.scalar_tensor_tensor(us, csum[:, g, :], 1.0 / w, us, ALU.mult, ALU.subtract).then_inc(dif_done, 1)

            head_norm1(0)
            take_state(0)
            products(1)
            carried(0)
            carried(1)
            head_norm2(0)
            take_heads(0)
            head_norm1(1)
            take_state(1)
            products(2)
            carried(2)
            carried(3)
            head_norm2(1)
            take_heads(1)
            take_last(0)
            head_norm1(2)
            take_state(2)
            products(3)
            head_norm2(2)
            pool_diff(0)
            carried(4)
            carried(5)
            pool_diff(1)
            take_heads(2)
            take_last(1)
            pool_diff(2)
            pool_diff(3)
            head_norm1(3)
            take_state(3)
            head_norm2(3)
            carried(6)
            take_heads(3)

            def take_logits(t):
                bk = full()
                V.tensor_copy(rt[:, t, 0:20], bk[0:TR, 0:20]).then_inc(dve_free, 1)

            def residual(t, signal, logits=False):
                for q in range(2):
                    if q == 1 and logits:
                        take_logits(t - 2)
                        if t == NT - 1:
                            dve.wait_ge(dve_free, nf[0])
                            choose(0)
                    bk = full()
                    x = xn[0:TR, t, q * 512:q * 512 + 512]
                    V.scalar_tensor_tensor(x, x, ALPHA, bk[0:TR, :], ALU.mult, ALU.add).then_inc(dve_free, 1)
                    dve.wait_ge(dve_free, nf[0])
                    if q == 0:
                        statistics(t, 0)
                norm(t, signal, first_known=True)

            dve.wait_ge(gb_in, 32)
            residual(0, x1_ready)
            carried(7)
            residual(1, x1_ready)
            bk = full()
            ck = P[0:NS, 10964:10964 + 512]
            link(V.tensor_tensor(v4(ck), v4(bk[0:NS, :]), b4(sg8[:, 16:20]), ALU.mult))
            V.tensor_tensor(vsn, vsn, ck, ALU.add).then_inc(dve_free, 1)
            dve.wait_ge(dve_free, nf[0])
            link(V.tensor_tensor(v4(vsn), v4(vsn), b4(sg8[:, 40:44]), ALU.mult))
            for h in range(H):
                last = V.bn_stats(hst[0:NS, h, :], vsn[:, h * HD:h * HD + HD])
            link(last)
            for h in range(H):
                last = V.bn_aggr(hagg[0:NS, h, :], hst[0:NS, h, :])
            last.then_inc(hs_var, 1)
            dve.wait_ge(hs_rstd, H + 1)
            dve.wait_ge(hs_var, H + 1)
            for h in range(H):
                x = vsn[:, h * HD:h * HD + HD]
                last = V.tensor_scalar(x, x, hagg[0:NS, h, 0:1], den[0:NS, 1, h:h + 1], ALU.subtract, ALU.mult)
            last.then_inc(hs_ready, 1)
            residual(2, x1_ready)
            bk = full()
            for h in range(H):
                last = V.scalar_tensor_tensor(mixT[:, 4 + h, NP_:NTOK], bk[:, h * NS:h * NS + NS], colv[:, 4 + h:5 + h], sgT[:, h, NP_:NTOK], ALU.mult, ALU.mult)
            last.then_inc(dve_free, 1)
            residual(3, x1_ready)
            residual(4, x1_ready)

            NQ = NT * 4

            def finish_probs(n):
                dve.wait_ge(act_free, at["attend", n])
                s = n % 4
                link(V.reciprocal(mx4[0:TR, 8 + s:9 + s], mx4[0:TR, 4 + s:5 + s]))
                V.tensor_scalar(Er[0:TR, s, :], Er[0:TR, s, :], mx4[0:TR, 8 + s:9 + s], None, ALU.mult).then_inc(prob_ready, 1)

            def sample_scores(b):
                dve.wait_ge(kq_done, 2 * b + 2)
                V.tensor_reduce(sS[:, :, 4 * b:4 * b + 4], kvr[:, b % 3].rearrange("p m (h e) -> p m h e", h=4), AX, ALU.add).then_inc(k_used, 1)

            sample_scores(0)
            sample_scores(1)
            later = (3, 7, 11, 15, 17, 18)
            for n in range(NQ):
                k = at["attend", n] - 1
                dve.wait_ge(act_full, k + 1)
                V.tensor_reduce(mx4[0:TR, n % 4:n % 4 + 1], RING_A[k % 3][0:TR, 0:NM], AX, ALU.max, negate=True).then_inc(nmax_done, 1)
                if n >= 1:
                    finish_probs(n - 1)
                if n in later:
                    sample_scores(2 + later.index(n))
            finish_probs(NQ - 1)
            bk = full()
            assert nf[0] == at["sample scores"]
            V.tensor_reduce(mx4[0:32, 0:1], bk[0:32, 0:NM], AX, ALU.max, negate=True).then_inc(s_nmax, 1)
            dve.wait_ge(s_exp, 1)
            V.reciprocal(mx4[0:32, 8:9], mx4[0:32, 4:5]).then_inc(dve_free, 1)
            dve.wait_ge(dve_free, nf[0])
            V.tensor_scalar(Es, Es, mx4[0:32, 8:9], None, ALU.mult).then_inc(s_prob, 1)
            bk = full()
            dve.wait_ge(paz_zero, 1)
            for m in range(2):
                diag = paz[:, m].rearrange("p r c -> p (r c)")[:, 0:32 * 32:33]
                last = V.tensor_copy(diag, bk[:, m * 32:m * 32 + 32])
            last.then_inc(dve_free, 1)
            bk = full()
            dve.wait_ge(sn_out, 16)
            V.tensor_copy(ctxs, bk[0:32, 0:CE]).then_inc(dve_free, 1)
            bk = full()
            for ec in range(2):
                src = bk[:, ec * 32:ec * 32 + 32].rearrange("p (b h) -> p h b", h=4)
                last = V.tensor_copy(ctxT.rearrange("p (h e) c -> p h e c", e=2)[:, :, ec, NP_:NTOK], src)
            last.then_inc(dve_free, 1)

            def routing(n):
                a0, a1 = ROUTED[n]
                r, T = rt[:, a0:a1, :], a1 - a0
                one = {name: r[:, :, 88 + i:89 + i] for i, name in enumerate(("gmax", "m1", "m2", "acc", "pg", "xx"))}
                return r, T, one

            def choose(n):
                r, T, one = routing(n)
                gmax, m1, m2, acc = one["gmax"], one["m1"], one["m2"], one["acc"]
                g, e16, gx, og, o1, o2, ein = [r[:, :, lo:hi] for lo, hi in ((0, 4), (4, 20), (20, 24), (24, 28), (28, 32), (32, 36), (36, 40))]
                O1, O2, tmp = [r[:, :, lo:lo + 16].rearrange("p t (g j) -> p t g j", g=NG) for lo in (40, 56, 72)]
                sc4 = lambda x: x.broadcast_to([TR, T, 4])
                by_group = lambda x: x.unsqueeze(3).broadcast_to([TR, T, NG, EG])
                by_expert = lambda x: x.unsqueeze(2).broadcast_to([TR, T, NG, EG])
                rank = con[0:TR, 312:316].unsqueeze(1).broadcast_to([TR, T, 4])

                def first_of(x):
                    link(V.tensor_tensor(x, x, rank, ALU.mult))
                    link(V.tensor_reduce(acc, x, AX, ALU.max))
                    link(V.tensor_tensor(x, x, sc4(acc), ALU.is_equal))

                link(V.tensor_reduce(gmax, g, AX, ALU.max))
                V.tensor_tensor(gx, g, sc4(gmax), ALU.subtract).then_inc(rt_dve, 1)
                link(V.tensor_tensor(og, g, sc4(gmax), ALU.is_equal))
                first_of(og)
                link(V.tensor_tensor(tmp, e16.rearrange("p t (g j) -> p t g j", g=NG), by_group(og), ALU.mult))
                link(V.tensor_reduce(ein, tmp.rearrange("p t g j -> p t j g"), AX, ALU.add))
                link(V.tensor_reduce(m1, ein, AX, ALU.max))
                link(V.tensor_tensor(o1, ein, sc4(m1), ALU.is_equal))
                first_of(o1)
                link(V.scalar_tensor_tensor(ein, o1, BIG, ein, ALU.mult, ALU.add))
                link(V.tensor_reduce(m2, ein, AX, ALU.max))
                V.tensor_tensor(one["xx"], m2, m1, ALU.subtract).then_inc(rt_dve, 1)
                link(V.tensor_tensor(o2, ein, sc4(m2), ALU.is_equal))
                first_of(o2)
                V.tensor_tensor(O1, by_group(og), by_expert(o1), ALU.mult)
                link(V.tensor_tensor(O2, by_group(og), by_expert(o2), ALU.mult))
                a0, a1 = ROUTED[n]
                V.tensor_tensor(Mb16[:, a0:a1, :], r[:, :, 40:56], r[:, :, 56:72], ALU.add).then_inc(mask_ready, 1)

            def gates(n):
                r, T, one = routing(n)
                pg, xx = one["pg"], one["xx"]
                g1, g2 = [tokg[:, ROUTED[n][0]:ROUTED[n][1], k, 1:2] for k in range(2)]
                dve.wait_ge(rt_act, 2 * n + 2)
                link(V.tensor_reduce(pg, r[:, :, 20:24], AX, ALU.add))
                link(V.scalar_tensor_tensor(pg, xx, 1.0, pg, ALU.add, ALU.mult))
                link(V.reciprocal(g1, pg))
                link(V.tensor_tensor(g2, g1, xx, ALU.mult))

            def list_rows(n):
                a0, a1 = ROUTED[n]
                r, T, one = routing(n)
                bk = full()
                base = con[0:TR, 296:312].unsqueeze(1).broadcast_to([TR, T, NE])
                tmp = r[:, :, 72:88]
                last = V.scalar_tensor_tensor(tmp, bk[0:TR, a0 * NE:a1 * NE].rearrange("p (t e) -> p t e", t=T), float(NE), base, ALU.mult, ALU.add)
                if a1 == NT:
                    last = V.tensor_reduce(most[0:1, :], bk[0:1, NT * NE:(NT + 1) * NE], AX, ALU.max)
                last.then_inc(dve_free, 1)
                dve.wait_ge(dve_free, nf[0])
                both = r[:, :, 40:72].rearrange("p t (k e) -> p t k e", k=2)
                link(V.tensor_tensor(both, both, tmp.unsqueeze(2).broadcast_to([TR, T, 2, NE]), ALU.mult))
                link(V.tensor_reduce(r[:, :, 89:91], both, AX, ALU.add))
                V.tensor_copy(dst[:, :, a0:a1], r[:, :, 89:91].rearrange("p t k -> p k t")).then_inc(dst_ready, 1)

            dve.wait_ge(gb_in, 64)
            for t in range(NT):
                residual(t, x2_ready, logits=t >= 2)
            gates(0)
            list_rows(0)
            take_logits(NT - 2)
            dve.wait_ge(dve_free, nf[0])
            choose(1)
            gates(1)
            list_rows(1)
            take_logits(NT - 1)
            dve.wait_ge(dve_free, nf[0])
            choose(2)
            gates(2)
            list_rows(2)
            link(V.tensor_scalar(most[:, :], most[:, :], float(C), None, ALU.is_gt))
            V.tensor_copy(flag[0:1, 0:1], most[:, :]).then_inc(flag_ready, 1)

            GU = [ps[2], ps[3], ps[6]]

            def expert_in(e, s):
                dve.wait_ge(xgT_full, e * 2 + 2)
                V.tensor_copy(xgT[:, s, 4:8, :], ps[1][:, :].rearrange("p (k c) -> p k c", k=4)).then_inc(xgT_dve, 1)

            def expert_hidden(e, s):
                dve.wait_ge(sgm_ready, e + 1)
                x = sgm[:, 0, :]
                V.tensor_scalar(x, x, 1.0, None, ALU.add).then_inc(hsteps, 1)
                dve.wait_ge(hsteps, e * 3 + 1)
                V.reciprocal(x, x).then_inc(hsteps, 1)
                dve.wait_ge(hsteps, e * 3 + 2)
                V.tensor_tensor(x, x, GU[s][:, 0:2 * C], ALU.mult).then_inc(hsteps, 1)
                dve.wait_ge(hsteps, e * 3 + 3)
                V.tensor_tensor(hh[:, s].rearrange("p f c -> p (f c)"), x, GU[s][:, 2 * C:4 * C], ALU.mult).then_inc(hh_ready, 1)

            def expert_out(e, s, k):
                dve.wait_ge(y_full, e + 1)
                if not (isinstance(k, int) and k == 0):
                    dve.wait_ge(y_out[s], k * 16)
                dve.wait_ge(gate_set, e + 1)
                V.tensor_scalar(ysb[:, s, 512:D], ps[5][:, :], gate3[:, s:s + 1], None, ALU.mult).then_inc(y_dve, 1)

            expert_in(0, 0)
            expert_in(1, 1)
            expert_hidden(0, 0)
            expert_hidden(1, 1)
            expert_in(2, 2)
            expert_out(0, 0, 0)

            def expert_step(e, u, i):
                expert_hidden(e, u)
                expert_in(e + 1, (u + 1) % 3)
                expert_out(e - 1, (u + 2) % 3, i - (1 if u == 0 else 0))

            for e in (2, 3):
                expert_step(e, e % 3, e // 3)
            with dve.Fori(1, 4) as i:
                for u in range(1, 4):
                    expert_step(i * 3 + u, u % 3, i + u // 3)
            for e in (13, 14):
                expert_step(e, e % 3, e // 3)
            expert_hidden(15, 0)
            expert_out(14, 2, 4)
            expert_out(15, 0, 5)

            over = dve.value_load(flag[0:1, 0:1], min_val=0, max_val=1)
            with dve.If(over > 0):
                dve.wait_ge(y_out[0], 96)
                with dve.Fori(0, NE * (NCH - 1)) as n:
                    dve.wait_ge(ov_t, n + 1)
                    V.tensor_copy(xgT[:, 0, 0:4, :], ps[0][:, :].rearrange("p (k c) -> p k c", k=4)).then_inc(ovs, 1)
                    V.tensor_copy(xgT[:, 0, 4:8, :], ps[1][:, :].rearrange("p (k c) -> p k c", k=4)).then_inc(ov_tc, 1)
                    dve.wait_ge(ov_sg, n + 1)
                    x = sgm[:, 0, :]
                    V.tensor_scalar(x, x, 1.0, None, ALU.add).then_inc(ovs, 1)
                    dve.wait_ge(ovs, n * 5 + 2)
                    V.reciprocal(x, x).then_inc(ovs, 1)
                    dve.wait_ge(ovs, n * 5 + 3)
                    V.tensor_tensor(x, x, GU[0][:, 0:2 * C], ALU.mult).then_inc(ovs, 1)
                    dve.wait_ge(ovs, n * 5 + 4)
                    V.tensor_tensor(hh[:, 0].rearrange("p f c -> p (f c)"), x, GU[0][:, 2 * C:4 * C], ALU.mult).then_inc(ov_h, 1)
                    dve.wait_ge(ov_y, n + 1)
                    V.tensor_scalar(ysb[:, 0, 0:512], ps[4][:, :], list1[:, 1:2], None, ALU.mult).then_inc(ovs, 1)
                    V.tensor_scalar(ysb[:, 0, 512:D], ps[5][:, :], list1[:, 1:2], None, ALU.mult).then_inc(ov_yc, 1)
                    dve.wait_ge(ov_out, n * 16 + 16)

            dve.wait_ge(gb_in, 96)
            for t in range(NT):
                dve.wait_ge(y_added[t], 32)
                if t < NT - 1:
                    norm(t, x3_centred, finish=False)
                else:
                    norm(t, x4_ready)

        @block.gpsimd
        def _(pool):
            G = nc.gpsimd
            steps = [0]

            def link(ins):
                steps[0] += 1
                ins.then_inc(pool_step, 1)
                pool.wait_ge(pool_step, steps[0])

            link(G.memset(half[:, :], -0.5))
            G.memset(onesb[:, :], 1.0)
            link(G.memset(wg[:, :, :], 0.0))
            win = a["w_in"][0].rearrange("(k p) c -> p k c", p=128)
            GO = PW + 4 * 512
            pool.dma_start(wg[:, :, 0:4], win[:, :, GO:GO + 4]).then_inc(wgr_in, 16)
            pool.dma_start(wg[:, :, 32:36], win[:, :, GO + 4:GO + 8]).then_inc(wgr_in, 16)
            pool.dma_start(wr[:, :, 0:4], a["w_gr"][0].rearrange("(k p) c -> p k c", p=128)).then_inc(wgr_in, 16)
            pool.dma_start(wr[:, :, 4:20], a["w_er"][0].rearrange("(k p) c -> p k c", p=128)).then_inc(wgr_in, 16)
            col = lambda ap: ap.rearrange("(c one) -> c one", one=1)
            pool.dma_start(colv[0:4, 8:9], col(a["b_i"][0])).then_inc(small_in, 16)
            pool.dma_start(colv[32:36, 9:10], col(a["b_f"][0])).then_inc(small_in, 16)
            pool.dma_start(colv[0:4, 10:11], col(a["b_gr"][0])).then_inc(small_in, 16)
            pool.dma_start(colv[4:20, 10:11], col(a["b_er"][0])).then_inc(small_in, 16)
            for g in range(4):
                pool.dma_start(colv[:, g:g + 1], col(a["pool_scale"][0, g * 128:g * 128 + 128])).then_inc(small_in, 16)
                pool.dma_start(colv[:, 4 + g:5 + g], col(a["mlstm_norm_g"][0, g * 128:g * 128 + 128])).then_inc(small_in, 16)
            pool.dma_start(poolw[:, :, :], a["pool_w"][0].rearrange("g c e -> c g e")).then_inc(small_in, 16)
            pool.dma_start(n0, a["state_mlstm_n"][0].rearrange("b h k -> b (h k)")).then_inc(st_in, 16)
            pool.dma_start(sg8[:, 28:32], a["state_mlstm_m"][0]).then_inc(st_in, 16)

            pows = [0]

            def norm_rstd():
                x = rstd[0:TR, pows[0] % NT:pows[0] % NT + 1]
                pows[0] += 1
                pool.wait_ge(var_ready, pows[0])
                link(G.tensor_scalar(x, agg[0:TR, 1:2], LN_EPS, None, ALU.add))
                G.tensor_tensor(x, x, half[0:TR, 0:1], ALU.pow).then_inc(rstd_ready, 1)

            for t in range(NT):
                norm_rstd()
            G.memset(uT[:, :, 0:PADC], 0.0)
            G.memset(pp[:, :, 0:PADC], 0.0)
            G.memset(hn[:, :, :, :], 1.0)
            G.memset(gcol[:, :], 1.0)
            G.memset(vn[:, :, :, HD:HD + 1], 1.0)
            G.memset(tokz, 0.0).then_inc(memset_done, 1)
            pool.wait_ge(memset_done, 1)
            pool.dma_start(lst_d.rearrange("(p r) w -> p (r w)", p=128), tokz.bitcast(U32)).then_inc(lst_zero, 16)

            def masks(h):
                offs = [0]
                for t in range(NT):
                    offs.append(offs[-1] + NP_ - t * TR)
                for t in range(NT):
                    pool.wait_ge(dve_free, at["scores", h, t])
                    r = rows_of(t)
                    blk = pst[0:r, offs[t]:offs[t] + r]
                    G.affine_select(blk, blk, pattern=[[1, r]], compare_op=ALU.is_ge, fill=0.0, base=0, channel_multiplier=-1).then_inc(sel_done, 1)

            def head_rstd(h, n, m):
                pool.wait_ge(hs_var, h + 1)
                link(G.tensor_scalar(den[0:n, 1, 0:m], hagg[0:n, 0:m, 1:2].rearrange("p t c -> p (t c)"), LN_EPS, None, ALU.add))
                G.tensor_tensor(den[0:n, 1, 0:m], den[0:n, 1, 0:m], half[0:n, 0:m], ALU.pow).then_inc(hs_rstd, 1)

            def state_out(h):
                pool.wait_ge(dve_free, at["state", h])
                pool.dma_start(o_pC[0, 0, h], Cout[:, h % 2, 0:HD]).then_inc(c_out[h % 2], 16)
                pool.dma_start(o_pn[0, 0, h:h + 1], Cout[0:1, h % 2, HD:2 * HD]).then_inc(c_out[h % 2], 16)

            def load_state(b):
                i = BUF[b]
                if earlier(b) > 0:
                    pool.wait_ge(c_store[i], 16 * earlier(b))
                pool.dma_start(Cs[i], a["state_mlstm_C"][0, b].rearrange("h v k -> v h k")).then_inc(c_in[i], 16)
                pool.dma_start(qk_b[i], qk_d[b].partition_broadcast(128)).then_inc(c_in[i], 16)

            def update_state(b):
                pool.wait_ge(cq_done, b + 1)
                wv = wcb[:, b, :].unsqueeze(2).broadcast_to([128, H, HD])
                vv = vsT[:, :, b:b + 1].broadcast_to([128, H, HD])
                c, k = Cs[BUF[b]], Ck_b[BUF[b]]
                G.tensor_tensor(c, c, wv, ALU.mult)
                link(G.tensor_tensor(k, k, vv, ALU.mult))
                G.tensor_tensor(c, c, k, ALU.add).then_inc(cupd_done, 1)
                pool.wait_ge(cupd_done, b + 1)
                pool.dma_start(o_sC[0, b].rearrange("h v k -> v h k"), c).then_inc(c_store[BUF[b]], 16)

            def window_sums(g):
                pool.wait_ge(act_free, at["u", 0])
                if g == 1:
                    pool.wait_ge(dif_done, 1)
                add_windows(G.tensor_tensor, g, link).then_inc(usum_done, 1)

            pool.wait_ge(rows_dve, 1)
            pool.dma_start(o_pm[0, 0].rearrange("(c one) -> c one", one=1), colv[0:4, 11:12]).then_inc(out_done, 16)
            masks(0)
            pool.wait_ge(snat_ready, 1)
            pool.dma_start(qk_d[:, 0:512], qsn).then_inc(bounce, 16)
            pool.dma_start(qk_d[:, 512:1024], ksn).then_inc(bounce, 16)
            pool.dma_start(swc_d, sg8[:, 16:20]).then_inc(bounce, 16)
            pool.dma_start(o_sn[0].rearrange("b h k -> b (h k)"), n0).then_inc(sn_out, 16)
            pool.dma_start(o_sm[0], sg8[:, 8:12]).then_inc(out_done, 16)
            pool.wait_ge(bounce, 48)
            pool.dma_start(wcb[:, :, :].rearrange("p b h -> p (b h)"), swc_d.rearrange("b h -> (b h)").partition_broadcast(128)).then_inc(bounce, 16)
            pool.wait_ge(bounce, 64)
            pool.wait_ge(lst_zero, 16)
            load_state(0)
            load_state(1)
            head_rstd(0, TR, NT)
            masks(1)
            for h in (0, 1):
                update_state(2 * h)
                update_state(2 * h + 1)
                load_state(2 * h + 2)
                load_state(2 * h + 3)
                state_out(h)
                head_rstd(h + 1, TR, NT)
                masks(h + 2)
            window_sums(0)
            window_sums(1)
            update_state(4)
            update_state(5)
            load_state(6)
            state_out(2)
            head_rstd(3, TR, NT)
            state_out(3)
            update_state(6)

            def norm_vectors(gname, bname):
                pool.dma_start(gb[:, 0, :], a[gname][0].partition_broadcast(128)).then_inc(gb_in, 16)
                pool.dma_start(gb[:, 1, :], a[bname][0].partition_broadcast(128)).then_inc(gb_in, 16)

            for i in range(2):
                pool.wait_ge(c_out[i], 64)
            norm_vectors("ln1_g", "ln1_b")
            load_state(7)
            pool.wait_ge(dve_free, at["last u", 1])
            pool.dma_start(o_ppool[0, 0], un[0:NPOOL, :]).then_inc(un_out, 16)
            pool.dma_start(o_spool[0, :, NPOOL - 1, :], un[NPOOL:NPOOL + NS, :]).then_inc(un_out, 16)
            pool.dma_start(o_spool[0, :, 0:NPOOL - 1, :], a["cache_pool"][0, :, 1:NPOOL, :]).then_inc(un_out, 16)
            norm_rstd()
            update_state(7)
            norm_rstd()
            head_rstd(4, NS, H)
            for t in range(3):
                norm_rstd()
            pool.wait_ge(x1_ready, NT)
            norm_vectors("ln2_g", "ln2_b")
            pool.wait_ge(act_free, at["sample q"])
            pool.dma_start(sq2_d, qs2).then_inc(sq2_out, 16)
            for b in range(NS):
                pool.wait_ge(kv_in[b % 3], 16 * (b // 3 + 1))
                for hf in range(2):
                    pool.wait_ge(qb_in[hf], 16 * (b + 1))
                    x = kvr[:, b % 3, :, hf * 512:hf * 512 + 512]
                    G.tensor_tensor(x, x, qb[:, hf * 512:hf * 512 + 512].unsqueeze(1).broadcast_to([128, 2, 512]), ALU.mult).then_inc(kq_done, 1)
            pool.wait_ge(sq2_out, 16)
            G.memset(paz, 0.0).then_inc(paz_zero, 1)
            for t in range(NT):
                norm_rstd()
                pool.wait_ge(x2_ready, t + 1)
                pool.dma_start(x2_d[t * TR:t * TR + TR, :], xn[0:TR, t, :]).then_inc(x2_out, 16)
            norm_vectors("ln3_g", "ln3_b")

            pool.wait_ge(dve_full, at["sample context"])
            G.iota(tokg[:, :, :, 0].bitcast(I32), pattern=[[TR, NT], [0, 2]], base=0, channel_multiplier=1).then_inc(tok_ready, 1)
            pool.wait_ge(tok_ready, 1)
            for t in range(NT):
                for n, (a0, a1) in enumerate(ROUTED):
                    if t == a0:
                        pool.wait_ge(dst_ready, n + 1)
                for k in range(2):
                    pool.indirect_dma_start(out=lst_d, out_offset=bass.IndirectOffsetOnAxis(ap=dst[:, k, t:t + 1], axis=0),
                                            in_=tokg[:, t, k, :].bitcast(U32), in_offset=None).then_inc(lst_out, 16)
            pool.wait_ge(lst_out, 16 * 2 * NT)
            pool.dma_start(lists.bitcast(U32), lst_e[0:C, :, :]).then_inc(idx_in, 16)
            pool.wait_ge(idx_in, 16)
            pool.wait_ge(x2_out, 16 * NT)
            for e in range(NE):
                s = e % 3
                if e >= 3:
                    pool.wait_ge(xgT_full, 2 * (e - 2))
                pool.indirect_dma_start(out=xg[:, s, :], out_offset=None, in_=x2_d,
                                        in_offset=bass.IndirectOffsetOnAxis(ap=lists[:, e, 0:1].bitcast(U32), axis=0)).then_inc(xg_in[s], 16)
                if e >= 3:
                    pool.wait_ge(y_act, e - 2)
                    pool.wait_ge(y_dve, e - 2)
                G.tensor_copy(gate3[:, s:s + 1], lists[:, e, 1:2]).then_inc(gate_set, 1)

            pool.wait_ge(flag_ready, 1)
            over = pool.value_load(flag[0:1, 0:1], min_val=0, max_val=1)
            with pool.If(over > 0):
                pool.wait_ge(xgT_full, 2 * NE)
                with pool.Fori(0, NE * (NCH - 1)) as n:
                    pool.wait_ge(ov_idx, n * 16 + 16)
                    G.tensor_tensor(turn[:, 0:1], turn[:, 1:2], turn[:, 1:2], ALU.mult).then_inc(ov_turn, 1)
                    pool.indirect_dma_start(out=xg[:, 0, :], out_offset=None, in_=x2_d,
                                            in_offset=bass.IndirectOffsetOnAxis(ap=list1[:, 0:1].bitcast(U32), axis=0)).then_inc(ov_x, 16)
                pool.wait_ge(ov_out, 16 * NE * (NCH - 1))

            for s in range(3):
                pool.wait_ge(y_out[s], 16 * (6 if s == 0 else 5))

            def finish(rows):
                def add(t, k):
                    pool.indirect_dma_start(out=xn[0:TR, t, :], out_offset=None, in_=y_d[0:rows, :],
                                            in_offset=bass.IndirectOffsetOnAxis(ap=dst[:, k, t:t + 1], axis=0),
                                            compute_op=ALU.add).then_inc(y_added[t], 16)

                pool.wait_ge(xa_ready, NT)
                for t in range(NT + 2):
                    if t < NT:
                        add(t, 0)
                    if t >= 2:
                        pool.wait_ge(y_added[t - 2], 16)
                        add(t - 2, 1)
                norm_rstd()
                for t in range(NT - 1):
                    norm_rstd()
                    pool.wait_ge(x3_scaled, t + 1)
                    x = xn[0:TR, t, :]
                    G.tensor_tensor(x, x, gb[0:TR, 1, :], ALU.add).then_inc(x3_ready, 1)

            before = pows[0], steps[0]
            with pool.If(over > 0):
                finish(NE * R)
            pows[0], steps[0] = before
            with pool.If(over < 1):
                finish(NE * C)


_OUTS = [(1, 512, 1024), (8, 1, 1024), (1, 1, 15, 512), (1, 1, 4, 128, 128), (1, 1, 4, 128), (1, 1, 4),
         (1, 1, 256, 4, 256), (1, 1, 256, 4, 256), (1, 8, 15, 512), (1, 8, 4, 128, 128), (1, 8, 4, 128), (1, 8, 4)]


def kernel(**inputs):
    import concourse.bacc as bacc
    from concourse.bass_utils import run_bass_kernel_spmd

    nc = bacc.Bacc("TRN2", target_bir_lowering=False, num_devices=1)
    arrays, aps = {}, {}
    for name, value in [*inputs.items(), ("consts", constants())]:
        value = np.ascontiguousarray(value)
        arrays[f"in_{name}"] = value
        aps[name] = nc.dram_tensor(f"in_{name}", value.shape, mybir.dt.from_np(value.dtype), kind="ExternalInput").ap()
    outs = [nc.dram_tensor(f"out_{i}", shape, F32, kind="ExternalOutput").ap() for i, shape in enumerate(_OUTS)]
    layer_kernel(nc, aps, outs)
    r = run_bass_kernel_spmd(nc, [arrays], core_ids=[0])
    return tuple(r.results[0][f"out_{i}"] for i in range(len(_OUTS)))
```
